# Optimizing a Trainium2 kernel written in Bass

```python
import math
import jax, jax.numpy as jnp
from jax import lax
import numpy as np

D_MODEL = 1024
BATCH = 1
SEQ = 512
DEPTH = 2

N_MIXERS = 2
HEAD_DIM = 64
V_DIM = 2 * HEAD_DIM
N_HEADS = D_MODEL // V_DIM
QK_WIDTH = N_HEADS * 2 * HEAD_DIM
V_WIDTH = N_HEADS * V_DIM
ROT_DIM = HEAD_DIM // 4
ROPE_THETA = 500000.0
Q_BLOCK = 128
CONV_WIDTH = 3
CONV_DIM = D_MODEL
D_FF = 4 * D_MODEL
EPS = 1e-6
N_ATTN = (DEPTH + 1) // 2
N_CONV = DEPTH // 2


def rmsnorm(x, g):
    xf = x.astype(jnp.float32)
    y = xf * lax.rsqrt(jnp.mean(xf * xf, axis=-1, keepdims=True) + EPS)
    return (y * g.astype(jnp.float32)).astype(x.dtype)

def rope_tables(seq_len):
    pos = jnp.arange(seq_len, dtype=jnp.float32)
    inv_freq = ROPE_THETA ** (-jnp.arange(0, ROT_DIM, 2, dtype=jnp.float32) / ROT_DIM)
    ang = pos[:, None] * inv_freq[None, :]
    return jnp.cos(ang), jnp.sin(ang)

def apply_partial_rope(t, cos, sin):
    half = ROT_DIM // 2
    x1 = t[..., :half].astype(jnp.float32)
    x2 = t[..., half:ROT_DIM].astype(jnp.float32)
    c = cos[None, :, None, None, :]
    s = sin[None, :, None, None, :]
    rot = jnp.concatenate([x1 * c - x2 * s, x2 * c + x1 * s], axis=-1).astype(t.dtype)
    return jnp.concatenate([rot, t[..., ROT_DIM:]], axis=-1)

def lambda_init_fn(layer_idx):
    return 0.8 - 0.6 * math.exp(-0.3 * layer_idx)

def diff_attention(x, w_qkv, w_o, lq1, lk1, lq2, lk2, subln_g, lambda_init):
    B, S, _ = x.shape
    qkv = x @ w_qkv
    q = qkv[..., :QK_WIDTH].reshape(B, S, N_HEADS, 2, HEAD_DIM)
    k = qkv[..., QK_WIDTH:2 * QK_WIDTH].reshape(B, S, N_HEADS, 2, HEAD_DIM)
    v = qkv[..., 2 * QK_WIDTH:].reshape(B, S, N_HEADS, V_DIM)
    cos, sin = rope_tables(S)
    q = apply_partial_rope(q, cos, sin) * (HEAD_DIM ** -0.5)
    k = apply_partial_rope(k, cos, sin)
    lam = (jnp.exp(jnp.sum(lq1.astype(jnp.float32) * lk1.astype(jnp.float32)))
           - jnp.exp(jnp.sum(lq2.astype(jnp.float32) * lk2.astype(jnp.float32)))
           + lambda_init)
    n_blocks = S // Q_BLOCK
    qb = q.reshape(B, n_blocks, Q_BLOCK, N_HEADS, 2, HEAD_DIM).transpose(1, 0, 2, 3, 4, 5)
    k32 = k.astype(jnp.float32)
    key_pos = jnp.arange(S)

    def block(args):
        q_i, i = args
        s = jnp.einsum('bqhcd,bkhcd->bhcqk', q_i.astype(jnp.float32), k32)
        q_pos = i * Q_BLOCK + jnp.arange(Q_BLOCK)
        mask = key_pos[None, :] <= q_pos[:, None]
        s = jnp.where(mask, s, -jnp.inf)
        p = jax.nn.softmax(s, axis=-1)
        a = p[:, :, 0] - lam * p[:, :, 1]
        return jnp.einsum('bhqk,bkhe->bqhe', a.astype(v.dtype), v)

    o = lax.map(block, (qb, jnp.arange(n_blocks)))
    o = o.transpose(1, 0, 2, 3, 4).reshape(B, S, N_HEADS, V_DIM)
    o = rmsnorm(o, subln_g) * (1.0 - lambda_init)
    return o.reshape(B, S, V_WIDTH) @ w_o

def short_conv(x, w_in, conv_w, w_out):
    h = x @ w_in
    b_gate = h[..., :CONV_DIM]
    c_gate = h[..., CONV_DIM:2 * CONV_DIM]
    u = c_gate * h[..., 2 * CONV_DIM:]
    up = jnp.pad(u, ((0, 0), (CONV_WIDTH - 1, 0), (0, 0)))
    S = x.shape[1]
    y = (conv_w[0] * up[:, 0:S] + conv_w[1] * up[:, 1:S + 1] + conv_w[2] * up[:, 2:S + 2])
    return (b_gate * y) @ w_out

def sq_relu_mlp(x, w_up, w_down):
    return jnp.square(jax.nn.relu(x @ w_up)) @ w_down

def first_inputs(seed: int = 0) -> dict:
    key = jax.random.key(seed)
    ks = jax.random.split(key, 20)
    f32 = jnp.float32
    D = D_MODEL

    def nrm(k, shape, scale):
        return jax.random.normal(k, shape, f32) * scale

    return {
        "x": nrm(ks[0], (BATCH, SEQ, D), 1.0),
        "attn_w_qkv": nrm(ks[1], (N_ATTN, D, 2 * QK_WIDTH + V_WIDTH), D ** -0.5),
        "attn_w_o": nrm(ks[2], (N_ATTN, V_WIDTH, D), V_WIDTH ** -0.5),
        "attn_lambda_q1": nrm(ks[3], (N_ATTN, HEAD_DIM), 0.1),
        "attn_lambda_k1": nrm(ks[4], (N_ATTN, HEAD_DIM), 0.1),
        "attn_lambda_q2": nrm(ks[5], (N_ATTN, HEAD_DIM), 0.1),
        "attn_lambda_k2": nrm(ks[6], (N_ATTN, HEAD_DIM), 0.1),
        "attn_subln_g": 1.0 + nrm(ks[7], (N_ATTN, V_DIM), 0.02),
        "conv_w_in": nrm(ks[8], (N_CONV, D, 3 * CONV_DIM), D ** -0.5),
        "conv_w": nrm(ks[9], (N_CONV, CONV_WIDTH, CONV_DIM), CONV_WIDTH ** -0.5),
        "conv_w_out": nrm(ks[10], (N_CONV, CONV_DIM, D), CONV_DIM ** -0.5),
        "mlp_w_up": nrm(ks[11], (DEPTH, D, D_FF), D ** -0.5),
        "mlp_w_down": nrm(ks[12], (DEPTH, D_FF, D), D_FF ** -0.5),
        "norm_mixer_pre": 1.0 + nrm(ks[13], (DEPTH, D), 0.02),
        "norm_mixer_post": 1.0 + nrm(ks[14], (DEPTH, D), 0.02),
        "norm_mlp_pre": 1.0 + nrm(ks[15], (DEPTH, D), 0.02),
        "norm_mlp_post": 1.0 + nrm(ks[16], (DEPTH, D), 0.02),
    }

def first_block(x, attn_w_qkv, attn_w_o, attn_lambda_q1, attn_lambda_k1, attn_lambda_q2,
              attn_lambda_k2, attn_subln_g, conv_w_in, conv_w, conv_w_out, mlp_w_up,
              mlp_w_down, norm_mixer_pre, norm_mixer_post, norm_mlp_pre, norm_mlp_post):
    for i in range(DEPTH):
        h = rmsnorm(x, norm_mixer_pre[i])
        j = i // N_MIXERS
        if i % N_MIXERS == 0:
            m = diff_attention(h, attn_w_qkv[j], attn_w_o[j], attn_lambda_q1[j],
                               attn_lambda_k1[j], attn_lambda_q2[j], attn_lambda_k2[j],
                               attn_subln_g[j], lambda_init_fn(i))
        else:
            m = short_conv(h, conv_w_in[j], conv_w[j], conv_w_out[j])
        x = x + rmsnorm(m, norm_mixer_post[i])
        h = rmsnorm(x, norm_mlp_pre[i])
        x = x + rmsnorm(sq_relu_mlp(h, mlp_w_up[i], mlp_w_down[i]), norm_mlp_post[i])
    return x


N_A_LAYERS = DEPTH // 2
N_B_LAYERS = DEPTH - N_A_LAYERS
DN_ALPHA = (2 * DEPTH) ** 0.25
DN_BETA = (8 * DEPTH) ** -0.25
SSD_EXPAND = 2
SSD_D_INNER = SSD_EXPAND * D_MODEL
SSD_HEAD_DIM = 64
SSD_N_HEADS = SSD_D_INNER // SSD_HEAD_DIM
SSD_N_GROUPS = 8
SSD_HEADS_PER_GROUP = SSD_N_HEADS // SSD_N_GROUPS
SSD_D_STATE = 128
SSD_CONV = 4
SSD_CHUNK = 128
SSD_GN = SSD_N_GROUPS * SSD_D_STATE
SSD_CONV_DIM = SSD_D_INNER + 2 * SSD_GN
SSD_IN_DIM = 2 * SSD_D_INNER + 2 * SSD_GN + SSD_N_HEADS
SSD_DT_MIN = 0.001
SSD_DT_MAX = 0.1
MLA_N_HEADS = D_MODEL // 128
MLA_Q_RANK = 384
MLA_KV_RANK = 256
MLA_NOPE = 128
MLA_ROPE = 64
MLA_V = 128
ROPE_THETA_2 = 10000.0
MAX_POS_OFFSET = 1024
FFN_HIDDEN = 2816
FFN_CONV = 3
LN_EPS = 1e-5
RMS_EPS = 1e-6


def layer_norm(x, g, b):
    xf = x.astype(jnp.float32)
    mu = jnp.mean(xf, axis=-1, keepdims=True)
    var = jnp.mean(jnp.square(xf - mu), axis=-1, keepdims=True)
    return ((xf - mu) * lax.rsqrt(var + LN_EPS) * g.astype(jnp.float32) + b.astype(jnp.float32)).astype(x.dtype)

def rms_norm(x, g, eps=RMS_EPS):
    xf = x.astype(jnp.float32)
    y = xf * lax.rsqrt(jnp.mean(xf * xf, axis=-1, keepdims=True) + eps)
    return (y * g.astype(jnp.float32)).astype(x.dtype)

def causal_depthwise_conv(x, w, b):
    width, ch = w.shape
    y = lax.conv_general_dilated(x, w[:, None, :].astype(x.dtype), window_strides=(1,),
                                 padding=[(width - 1, 0)],
                                 dimension_numbers=('NWC', 'WIO', 'NWC'),
                                 feature_group_count=ch)
    return y + b.astype(x.dtype)

def rope_tables_2(positions):
    inv_freq = 1.0 / (ROPE_THETA_2 ** (jnp.arange(0, MLA_ROPE, 2, dtype=jnp.float32) / MLA_ROPE))
    ang = positions.astype(jnp.float32)[..., None] * inv_freq
    return jnp.cos(ang), jnp.sin(ang)

def apply_rope(x, cos, sin):
    xf = x.astype(jnp.float32)
    x1, x2 = jnp.split(xf, 2, axis=-1)
    return jnp.concatenate([x1 * cos - x2 * sin, x2 * cos + x1 * sin], axis=-1).astype(x.dtype)

def ssd_chunked_scan(xs, dt, A, Bm, Cm):
    b, s = xs.shape[:2]
    nc = s // SSD_CHUNK

    def chunks(a):
        return jnp.moveaxis(a.reshape((b, nc, SSD_CHUNK) + a.shape[2:]), 1, 0)

    causal = jnp.tril(jnp.ones((SSD_CHUNK, SSD_CHUNK), dtype=bool))[None, :, :, None, None]

    def step(state, inp):
        xc, dtc, bc, cc = inp
        cum = jnp.cumsum(dtc * A, axis=1)
        seg = cum[:, :, None] - cum[:, None, :]
        decay = jnp.exp(jnp.where(causal, seg, -jnp.inf))
        cb = jnp.einsum('btgn,bsgn->btsg', cc, bc)
        w = cb[..., None] * decay * dtc[:, None]
        y = jnp.einsum('btsgk,bsgkp->btgkp', w, xc)
        y = y + jnp.einsum('btgn,bgkpn->btgkp', cc, state) * jnp.exp(cum)[..., None]
        w_end = jnp.exp(cum[:, -1:] - cum) * dtc
        state = (state * jnp.exp(cum[:, -1])[..., None, None]
                 + jnp.einsum('bsgk,bsgkp,bsgn->bgkpn', w_end, xc, bc))
        return state, y

    init = jnp.zeros((b, SSD_N_GROUPS, SSD_HEADS_PER_GROUP, SSD_HEAD_DIM, SSD_D_STATE), jnp.float32)
    _, y = lax.scan(step, init, (chunks(xs), chunks(dt), chunks(Bm), chunks(Cm)))
    return jnp.moveaxis(y, 0, 1).reshape(xs.shape)

def ssd_mixer(x, in_proj, conv_w, conv_b, dt_bias, A_log, D, norm_g, out_proj):
    b, s, _ = x.shape
    G, K, P, N = SSD_N_GROUPS, SSD_HEADS_PER_GROUP, SSD_HEAD_DIM, SSD_D_STATE
    zxbcdt = x @ in_proj
    z = zxbcdt[..., :SSD_D_INNER]
    xbc = zxbcdt[..., SSD_D_INNER:SSD_D_INNER + SSD_CONV_DIM]
    dt = zxbcdt[..., SSD_D_INNER + SSD_CONV_DIM:]
    xbc = jax.nn.silu(causal_depthwise_conv(xbc, conv_w, conv_b))
    xs = xbc[..., :SSD_D_INNER].reshape(b, s, G, K, P).astype(jnp.float32)
    Bm = xbc[..., SSD_D_INNER:SSD_D_INNER + SSD_GN].reshape(b, s, G, N).astype(jnp.float32)
    Cm = xbc[..., SSD_D_INNER + SSD_GN:].reshape(b, s, G, N).astype(jnp.float32)
    dt = jax.nn.softplus(dt.astype(jnp.float32) + dt_bias.astype(jnp.float32)).reshape(b, s, G, K)
    A = -jnp.exp(A_log.astype(jnp.float32)).reshape(G, K)
    y = ssd_chunked_scan(xs, dt, A, Bm, Cm)
    y = y + D.astype(jnp.float32).reshape(G, K)[..., None] * xs
    y = y.reshape(b, s, SSD_D_INNER) * jax.nn.silu(z.astype(jnp.float32))
    yg = y.reshape(b, s, G, SSD_D_INNER // G)
    yg = yg * lax.rsqrt(jnp.mean(yg * yg, axis=-1, keepdims=True) + LN_EPS)
    y = (yg.reshape(b, s, SSD_D_INNER) * norm_g.astype(jnp.float32)).astype(x.dtype)
    return y @ out_proj

def mla_shared_kv(h, kv_down_proj, kv_norm_g, kv_up_k, kv_up_v, cos, sin):
    b, s, _ = h.shape
    ckv_kr = h @ kv_down_proj
    c_kv = rms_norm(ckv_kr[..., :MLA_KV_RANK], kv_norm_g)
    k_rope = apply_rope(ckv_kr[..., MLA_KV_RANK:], cos, sin)
    k_nope = (c_kv @ kv_up_k).reshape(b, s, MLA_N_HEADS, MLA_NOPE)
    v = (c_kv @ kv_up_v).reshape(b, s, MLA_N_HEADS, MLA_V)
    return k_nope, k_rope, v

def mla_attention(h, q_down, q_norm_g, q_up, out_proj, k_nope, k_rope, v, cos, sin):
    b, s, _ = h.shape
    c_q = rms_norm(h @ q_down, q_norm_g)
    q = (c_q @ q_up).reshape(b, s, MLA_N_HEADS, MLA_NOPE + MLA_ROPE)
    q_nope = q[..., :MLA_NOPE]
    q_rope = apply_rope(q[..., MLA_NOPE:], cos[:, :, None], sin[:, :, None])
    nb = s // Q_BLOCK
    scale = (MLA_NOPE + MLA_ROPE) ** -0.5
    key_idx = jnp.arange(s)

    def to_blocks(a):
        return jnp.moveaxis(a.reshape((b, nb, Q_BLOCK) + a.shape[2:]), 1, 0)

    def attend_block(args):
        qn, qr, blk = args
        scores = (jnp.einsum('bqhd,bkhd->bhqk', qn, k_nope)
                  + jnp.einsum('bqhr,bkr->bhqk', qr, k_rope)).astype(jnp.float32) * scale
        q_idx = blk * Q_BLOCK + jnp.arange(Q_BLOCK)
        scores = jnp.where(key_idx[None, :] <= q_idx[:, None], scores, -jnp.inf)
        p = jax.nn.softmax(scores, axis=-1).astype(v.dtype)
        return jnp.einsum('bhqk,bkhd->bqhd', p, v)

    o = lax.map(attend_block, (to_blocks(q_nope), to_blocks(q_rope), jnp.arange(nb)))
    o = jnp.moveaxis(o, 0, 1).reshape(b, s, MLA_N_HEADS * MLA_V)
    return o @ out_proj

def conv_ffn(h, up, conv_w, conv_b, down):
    u = causal_depthwise_conv(h @ up, conv_w, conv_b)
    g, val = jnp.split(u, 2, axis=-1)
    return (jax.nn.silu(g) * val) @ down

def second_inputs(seed: int = 0) -> dict:
    key = jax.random.key(seed)
    ks = jax.random.split(key, 32)
    f32 = jnp.float32

    def nrm(k, shape, scale):
        return jax.random.normal(k, shape, f32) * scale

    na, nbl, d = N_A_LAYERS, N_B_LAYERS, D_MODEL
    x = nrm(ks[0], (BATCH, SEQ, d), 1.0)
    offset = jax.random.randint(ks[1], (BATCH, 1), 0, MAX_POS_OFFSET, dtype=jnp.int32)
    positions = (offset + jnp.arange(SEQ, dtype=jnp.int32)[None, :]).astype(jnp.int32)

    u = jax.random.uniform(ks[2], (na, SSD_N_HEADS), f32)
    dt0 = jnp.exp(u * (math.log(SSD_DT_MAX) - math.log(SSD_DT_MIN)) + math.log(SSD_DT_MIN))
    dt0 = jnp.maximum(dt0, 1e-4)
    ssd_dt_bias = dt0 + jnp.log(-jnp.expm1(-dt0))
    ssd_A_log = jnp.log(jax.random.uniform(ks[3], (na, SSD_N_HEADS), f32, 1.0, 16.0))

    return {
        'x': x,
        'positions': positions,
        'ssd_in_proj': nrm(ks[4], (na, d, SSD_IN_DIM), d ** -0.5),
        'ssd_conv_w': nrm(ks[5], (na, SSD_CONV, SSD_CONV_DIM), SSD_CONV ** -0.5),
        'ssd_conv_b': nrm(ks[6], (na, SSD_CONV_DIM), 0.02),
        'ssd_dt_bias': ssd_dt_bias,
        'ssd_A_log': ssd_A_log,
        'ssd_D': 1.0 + nrm(ks[7], (na, SSD_N_HEADS), 0.1),
        'ssd_norm_g': 1.0 + nrm(ks[8], (na, SSD_D_INNER), 0.02),
        'ssd_out_proj': nrm(ks[9], (na, SSD_D_INNER, d), DN_BETA * SSD_D_INNER ** -0.5),
        'kv_down_proj': nrm(ks[10], (d, MLA_KV_RANK + MLA_ROPE), d ** -0.5),
        'kv_norm_g': 1.0 + nrm(ks[11], (MLA_KV_RANK,), 0.02),
        'kv_up_k': nrm(ks[12], (MLA_KV_RANK, MLA_N_HEADS * MLA_NOPE), MLA_KV_RANK ** -0.5),
        'kv_up_v': nrm(ks[13], (MLA_KV_RANK, MLA_N_HEADS * MLA_V), DN_BETA * MLA_KV_RANK ** -0.5),
        'q_down_proj': nrm(ks[14], (nbl, d, MLA_Q_RANK), d ** -0.5),
        'q_norm_g': 1.0 + nrm(ks[15], (nbl, MLA_Q_RANK), 0.02),
        'q_up_proj': nrm(ks[16], (nbl, MLA_Q_RANK, MLA_N_HEADS * (MLA_NOPE + MLA_ROPE)), MLA_Q_RANK ** -0.5),
        'attn_out_proj': nrm(ks[17], (nbl, MLA_N_HEADS * MLA_V, d), DN_BETA * (MLA_N_HEADS * MLA_V) ** -0.5),
        'ffn_up': nrm(ks[18], (DEPTH, d, 2 * FFN_HIDDEN), d ** -0.5),
        'ffn_conv_w': nrm(ks[19], (DEPTH, FFN_CONV, 2 * FFN_HIDDEN), FFN_CONV ** -0.5),
        'ffn_conv_b': nrm(ks[20], (DEPTH, 2 * FFN_HIDDEN), 0.02),
        'ffn_down': nrm(ks[21], (DEPTH, FFN_HIDDEN, d), DN_BETA * FFN_HIDDEN ** -0.5),
        'ln_mix_g': 1.0 + nrm(ks[22], (DEPTH, d), 0.02),
        'ln_mix_b': nrm(ks[23], (DEPTH, d), 0.02),
        'ln_ffn_g': 1.0 + nrm(ks[24], (DEPTH, d), 0.02),
        'ln_ffn_b': nrm(ks[25], (DEPTH, d), 0.02),
    }

def second_block(x, positions, ssd_in_proj, ssd_conv_w, ssd_conv_b, ssd_dt_bias, ssd_A_log, ssd_D,
              ssd_norm_g, ssd_out_proj, kv_down_proj, kv_norm_g, kv_up_k, kv_up_v, q_down_proj,
              q_norm_g, q_up_proj, attn_out_proj, ffn_up, ffn_conv_w, ffn_conv_b, ffn_down,
              ln_mix_g, ln_mix_b, ln_ffn_g, ln_ffn_b):
    cos, sin = rope_tables_2(positions)
    h = x
    shared_kv = None
    for i in range(DEPTH):
        if i < N_A_LAYERS:
            mix = ssd_mixer(h, ssd_in_proj[i], ssd_conv_w[i], ssd_conv_b[i], ssd_dt_bias[i],
                            ssd_A_log[i], ssd_D[i], ssd_norm_g[i], ssd_out_proj[i])
        else:
            j = i - N_A_LAYERS
            k_nope, k_rope, v = shared_kv
            mix = mla_attention(h, q_down_proj[j], q_norm_g[j], q_up_proj[j], attn_out_proj[j],
                                k_nope, k_rope, v, cos, sin)
        h = layer_norm(DN_ALPHA * h + mix, ln_mix_g[i], ln_mix_b[i])
        ff = conv_ffn(h, ffn_up[i], ffn_conv_w[i], ffn_conv_b[i], ffn_down[i])
        h = layer_norm(DN_ALPHA * h + ff, ln_ffn_g[i], ln_ffn_b[i])
        if i == N_A_LAYERS - 1:
            shared_kv = mla_shared_kv(h, kv_down_proj, kv_norm_g, kv_up_k, kv_up_v, cos, sin)
    return h


def setup_inputs(seed=0):
    out = dict(first_inputs(seed))
    for name, value in second_inputs(seed + 1).items():
        if name != "x":
            out[name + "_2"] = value
    return out


def reference(
    x, attn_w_qkv, attn_w_o, attn_lambda_q1, attn_lambda_k1, attn_lambda_q2, attn_lambda_k2,
    attn_subln_g, conv_w_in, conv_w, conv_w_out, mlp_w_up, mlp_w_down, norm_mixer_pre,
    norm_mixer_post, norm_mlp_pre, norm_mlp_post, positions_2, ssd_in_proj_2, ssd_conv_w_2,
    ssd_conv_b_2, ssd_dt_bias_2, ssd_A_log_2, ssd_D_2, ssd_norm_g_2, ssd_out_proj_2,
    kv_down_proj_2, kv_norm_g_2, kv_up_k_2, kv_up_v_2, q_down_proj_2, q_norm_g_2, q_up_proj_2,
    attn_out_proj_2, ffn_up_2, ffn_conv_w_2, ffn_conv_b_2, ffn_down_2, ln_mix_g_2, ln_mix_b_2,
    ln_ffn_g_2, ln_ffn_b_2,
):
    x = first_block(
        x, attn_w_qkv, attn_w_o, attn_lambda_q1, attn_lambda_k1, attn_lambda_q2, attn_lambda_k2,
        attn_subln_g, conv_w_in, conv_w, conv_w_out, mlp_w_up, mlp_w_down, norm_mixer_pre,
        norm_mixer_post, norm_mlp_pre, norm_mlp_post,
    )
    return second_block(
        x, positions_2, ssd_in_proj_2, ssd_conv_w_2, ssd_conv_b_2, ssd_dt_bias_2, ssd_A_log_2,
        ssd_D_2, ssd_norm_g_2, ssd_out_proj_2, kv_down_proj_2, kv_norm_g_2, kv_up_k_2,
        kv_up_v_2, q_down_proj_2, q_norm_g_2, q_up_proj_2, attn_out_proj_2, ffn_up_2,
        ffn_conv_w_2, ffn_conv_b_2, ffn_down_2, ln_mix_g_2, ln_mix_b_2, ln_ffn_g_2, ln_ffn_b_2,
    )


_drawn_inputs = setup_inputs


def setup_inputs(seed=0):
    import zlib

    import numpy as np

    out = dict(_drawn_inputs(seed))
    spreads = {}
    factors = {'attn_lambda_q2': 8.0,
     'norm_mlp_post': 3.092,
     'ssd_conv_b_2': 8.0,
     'ssd_D_2': 8.0,
     'ssd_norm_g_2': 8.0,
     'kv_norm_g_2': 8.0,
     'kv_up_k_2': 3.083,
     'q_down_proj_2': 2.676,
     'q_norm_g_2': 8.0,
     'q_up_proj_2': 2.731,
     'ffn_conv_b_2': 6.678}
    for name, (base, spread) in spreads.items():
        noise = np.random.default_rng([zlib.crc32(name.encode()), seed]).standard_normal(out[name].shape)
        drawn = base * np.exp(spread * noise) if base else spread * noise
        out[name] = __import__('jax').numpy.asarray(drawn.astype(out[name].dtype))
    for name, factor in factors.items():
        out[name] = (out[name] * factor).astype(out[name].dtype)
    return out
```

```python
import math
from contextlib import ExitStack, contextmanager

import numpy as np

import concourse.bass as bass
from concourse import mybir

F32 = mybir.dt.float32
F32R = mybir.dt.float32r
I32 = mybir.dt.int32
ACT = mybir.ActivationFunctionType
ALU = mybir.AluOpType
AX_X = mybir.AxisListType.X

P = 128
T = 512
TB = T // P
D = 1024
DT_ = D // P
HEADS = 8
NEG = -float(2 ** 100)
SEED = 8
SLOTS = 4
SLAB = 1024

HALF_ROT = 8
FF1 = 4096
LAMBDA_INIT = 0.8 - 0.6 * math.exp(-0.3 * 0)
EPS = 1e-6
DN_ALPHA = (2 * 2) ** 0.25
LN_EPS = 1e-5
SSD_INNER = 2048
GROUPS = 8
SSD_STATE = 128
SSD_H = 32
HPG = 4
PD = 64
FFN = 2816
FFN_T = FFN // P
FFN_HALVES = (12, 10)
MLA_NOPE, MLA_ROPE = 128, 64
KV_RANK, Q_RANK = 256, 384

TWO_PI = (6.28125, 0.0019350051879882812, 2 * math.pi - 6.28125 - 0.0019350051879882812)
PI_DOWN = 3.1415925
ROUND = 1.5 * 2 ** 23

TRI = {0: (0, 0), 1: (1, 0), 2: (2, 0), 3: (1, 384)}
TRI_W = (512, 512, 256)


def vector_columns():
    at, n = {}, 0
    for name, k in (("mix_pre", 16), ("mix_post", 16), ("mlp_pre", 16), ("mlp_post", 16), ("conv_w", 24),
                    ("subln", 1), ("ssd_w", 128), ("ssd_b", 32), ("ssd_norm", 16), ("ssd_D", 16),
                    ("A_log", 1), ("dt_bias", 1), ("kv_g", 2), ("q_g", 3), ("ffn_w", 264), ("ffn_b", 88),
                    ("ln_mix_g", 16), ("ln_mix_b", 16), ("ln_ffn_g", 16), ("ln_ffn_b", 16), ("inv_freq", 1)):
        at[name] = n
        n += k
    return at, n


def constant_columns():
    at, n = {}, 0
    for name, k in (("ident", P), ("ones", P), ("rot", P), ("rot2", P), ("mask", P), ("sel", HPG * P),
                    ("cos", T), ("sin", T), ("gmask", GROUPS)):
        at[name] = n
        n += k
    return at, n


class Stage:

    def __init__(self, name, iters, slabs, ahead):
        self.name, self.iters, self.slabs, self.ahead = name, iters, slabs, ahead
        self.base = None

    def place(self, uses):
        self.base = list(uses)
        self.per = [sum(s[0] == k for s in self.slabs) for k in range(SLOTS)]
        return [b + p * self.iters for b, p in zip(self.base, self.per)]

    def use(self, pos, i):
        slot = self.slabs[pos][0]
        return self.base[slot] + self.per[slot] * i + sum(s[0] == slot for s in self.slabs[:pos + 1])


@contextmanager
def loop(eng, n, start=0):
    if n - start == 1:
        yield start
    else:
        with eng.Fori(start, n) as i:
            yield i


SECTIONS = ("attention", "mlp 0", "conv", "mlp 1", "split", "ssd", "ffn 0", "mla", "ffn 1")


def program(nc, a, out, sections=SECTIONS):
    ctx = ExitStack()
    V, NV = vector_columns()
    C, NC = constant_columns()

    def sb(name, shape, dt=F32):
        return ctx.enter_context(nc.sbuf_tensor(name, shape, dt))

    xT = sb("xT", [P, DT_, T])
    acc = sb("acc", [P, DT_, T])
    stg = sb("stg", [P, SLOTS, SLAB])
    wh = sb("wh", [P, SLOTS, SLAB], F32R)
    wl = sb("wl", [P, SLOTS, SLAB], F32R)
    hh = sb("hh", [P, DT_, T], F32R)
    hl = sb("hl", [P, DT_, T], F32R)
    bh = sb("bh", [P, 16, T], F32R)
    bl = sb("bl", [P, 16, T], F32R)
    vec = sb("vec", [P, NV])
    con = sb("con", [P, C["mask"]])
    cr = sb("cr", [P, P + P + HPG * P], F32R)
    gmask = sb("gmask", [64, GROUPS])
    positions = sb("positions", [64, T], I32)
    tmp = sb("tmp", [P, 6, T])
    cb = sb("cb", [P, 3, T])
    diag = sb("diag", [P, T])
    sm = sb("sm", [P, 64])
    ps = ctx.enter_context(nc.psum_tensor("ps", [P, 8, T], F32))

    ident, ones = con[:, C["ident"]:C["ident"] + P], con[:, C["ones"]:C["ones"] + P]
    rot, rot2 = con[:, C["rot"]:C["rot"] + P], con[:, C["rot2"]:C["rot2"] + P]
    ident_r, mask_r = cr[:, 0:P], cr[:, P:2 * P]
    sel = cr[:, 2 * P:].rearrange("p (k m) -> p k m", k=HPG)
    stat4, rstd4, half4 = sm[:, 0:4], sm[:, 4:8], sm[:, 8:12]
    lam = sm[:, 12:13]
    mx, nm, den, inv = sm[:, 16:24], sm[:, 24:32], sm[:, 32:40], sm[:, 40:48]
    oss, ovar, orstd = sm[:, 48:52], sm[:, 52:56], sm[:, 56:60]
    subg = sm[:, 60:61]
    lam2 = sm[:, 61:63]

    def new(name):
        return ctx.enter_context(nc.semaphore(name))

    class s:
        landed = [new(f"landed{k}") for k in range(SLOTS)]
        hi_done = [new(f"hi_done{k}") for k in range(SLOTS)]
        lo_done = [new(f"lo_done{k}") for k in range(SLOTS)]
        multiplied = [new(f"multiplied{k}") for k in range(SLOTS)]
        bank_free = new("bank_free")
        const_in = new("const_in")
        x_in = new("x_in")
        const_r = new("const_r")
        stat_in = new("stat_in")
        stat_used = new("stat_used")
        var_done = new("var_done")
        rstd_done = new("rstd_done")
        diag_done = new("diag_done")
        bc_done = new("bc_done")
        normed = new("normed")
        x_new = new("x_new")
        h_new = new("h_new")
        h_hi = new("h_hi")
        h_lo = new("h_lo")
        acc_done = new("acc_done")
        out_done = new("out_done")
        squared = new("squared")
        hid_hi = new("hid_hi")
        hid_lo = new("hid_lo")
        conv_read = new("conv_read")
        ffn_scaled = new("ffn_scaled")
        ffn_tap = new("ffn_tap")
        ffn_gate = new("ffn_gate")
        ffn_silu = new("ffn_silu")
        ffn_hidden = new("ffn_hidden")
        c_copied = new("c_copied")
        conv_u = new("conv_u")
        conv_scaled = new("conv_scaled")
        conv_tap = new("conv_tap")
        gated = new("gated")
        lam_in = new("lam_in")
        lam_sum = new("lam_sum")
        lam_exp = new("lam_exp")
        lam_done = new("lam_done")
        raw_done = new("raw_done")
        rot_done = new("rot_done")
        rope_done = new("rope_done")
        qk_hi = new("qk_hi")
        qk_lo = new("qk_lo")
        vt_done = new("vt_done")
        v_hi = new("v_hi")
        v_lo = new("v_lo")
        scores_done = new("scores_done")
        max_done = new("max_done")
        negmax = new("negmax")
        exp_done = new("exp_done")
        inv_done = new("inv_done")
        weighed = new("weighed")
        combined = new("combined")
        at_done = new("at_done")
        at_hi = new("at_hi")
        at_lo = new("at_lo")
        pv_done = new("pv_done")
        o_sq = new("o_sq")
        o_var = new("o_var")
        o_rstd = new("o_rstd")
        o_norm = new("o_norm")
        ot_done = new("ot_done")
        ot_hi = new("ot_hi")
        ot_lo = new("ot_lo")
        ln_sum = new("ln_sum")
        centered = new("centered")
        ln_x = new("ln_x")
        dt_exp = new("dt_exp")
        dt_done = new("dt_done")
        cum_done = new("cum_done")
        cum_t = new("cum_t")
        cum_n = new("cum_n")
        cb_done = new("cb_done")
        cb_copied = new("cb_copied")
        g_sel = new("g_sel")
        decay_done = new("decay_done")
        e_done = new("e_done")
        w_done = new("w_done")
        w_hi = new("w_hi")
        w_lo = new("w_lo")
        y_done = new("y_done")
        y_skip = new("y_skip")
        y_gate = new("y_gate")
        y_sq = new("y_sq")
        y_stat = new("y_stat")
        y_var = new("y_var")
        y_rstd = new("y_rstd")
        y_diag = new("y_diag")
        y_bc = new("y_bc")
        y_norm = new("y_norm")
        sc_scaled = new("sc_scaled")
        sc_conv = new("sc_conv")
        y_copied = new("y_copied")
        y_hi = new("y_hi")
        y_lo = new("y_lo")
        sc_tap = new("sc_tap")
        sc_gate = new("sc_gate")
        sc_silu = new("sc_silu")
        bc_hi = new("bc_hi")
        bc_lo = new("bc_lo")
        x_nat = new("x_nat")
        x_hi = new("x_hi")
        x_lo = new("x_lo")
        z_gate = new("z_gate")
        z_silu = new("z_silu")
        kvq_copied = new("kvq_copied")
        kvq_norm = new("kvq_norm")
        kvq_hi = new("kvq_hi")
        kvq_lo = new("kvq_lo")
        m_lo = new("m_lo")
        m_out_lo = new("m_out_lo")
        m_scores = new("m_scores")
        m_combined = new("m_combined")
        m_at = new("m_at")
        m_at_lo = new("m_at_lo")
        m_pv = new("m_pv")
        m_raw = new("m_raw")
        m_rot = new("m_rot")
        m_negmax = new("m_negmax")
        m_exp = new("m_exp")
        m_at_hi = new("m_at_hi")
        m_hi = new("m_hi")
        m_rope = new("m_rope")
        m_out_hi = new("m_out_hi")
        m_max = new("m_max")
        m_inv = new("m_inv")
        ang_done = new("ang_done")
        tab_done = new("tab_done")
        kr_rot = new("kr_rot")
        kr_done = new("kr_done")

    def v(name, j=0):
        if isinstance(j, int):
            return vec[:, V[name] + j:V[name] + j + 1]
        return vec[:, bass.ds(j + V[name], 1)]

    def tile(buf, m):
        if isinstance(m, int):
            return buf[:, m, :]
        return buf[:, bass.ds(m, 1), :].rearrange("p a t -> p (a t)")

    def columns(w, col, width, k0, k):
        sl = slice(col, col + width) if isinstance(col, int) else bass.ds(col, width)
        return w[k0 * P:(k0 + k) * P, sl].rearrange("(k p) c -> p k c", p=P)

    def address(i, step, col):
        return (i * step) * P if isinstance(col, int) and col == 0 else i * (step * P) + col

    stream = []

    def stage(name, iters, slabs, ahead):
        stream.append(Stage(name, iters, slabs, ahead))
        return stream[-1]

    def square_stage(name, w, m_tiles, per, kparts, col0=0, krow0=0):
        slabs, slot = [], 0
        for t in range(per):
            k0 = krow0
            for k in kparts:
                slabs.append((slot % SLOTS, k, P,
                              lambda i, t=t, k0=k0, k=k: columns(w, (i * per + t) * P + col0, P, k0, k)))
                k0 += k
                slot += 1
        return stage(name, m_tiles // per, slabs, SLOTS)

    st_mlp, st_ffn = {}, {}
    for section in sections:
        if section == "attention":
            st_att = stage("attention", HEADS, [
                (c, DT_, P, lambda i, c=c: columns(a["attn_w_qkv"][0], i * P + c * D, P, 0, DT_))
                for c in range(3)], 3)
            st_o = square_stage("attention out", a["attn_w_o"][0], DT_, 4, (8,))
        elif section == "conv":
            st_conv = stage("conv", 4, [
                (n % 3, DT_, P, lambda i, c=c: columns(a["conv_w_in"][0], address(i, 2, c), P, 0, DT_))
                for n, c in enumerate((D, 2 * D, 0, D + P, 2 * D + P, P))], 3)
            st_cout = square_stage("conv out", a["conv_w_out"][0], DT_, 4, (8,))
        elif section.startswith("mlp"):
            layer = int(section[-1])
            for half in range(2):
                st_mlp[layer, half] = (
                    square_stage("up", a["mlp_w_up"][layer], 16, 4, (8,), col0=half * 2048),
                    square_stage("down", a["mlp_w_down"][layer], DT_, 2, (8, 8), krow0=half * 16))
        elif section.startswith("ffn"):
            layer = int(section[-1])
            for half, tiles in enumerate(FFN_HALVES):
                t0 = half * FFN_HALVES[0]
                st_ffn[layer, half] = (
                    stage("gated up", tiles // 2, [
                        (n, DT_, P, lambda i, n=n, t0=t0, layer=layer: columns(
                            a["ffn_up_2"][layer], (2 * i + (n // 2 + n % 2 * FFN_T + t0)) * P, P, 0, DT_))
                        for n in range(4)], SLOTS),
                    square_stage("gated down", a["ffn_down_2"][layer], DT_, 2, (tiles // 2, tiles // 2), krow0=t0))
        elif section == "mla":
            st_lat = stage("latents", 1, [(0, DT_, P, lambda i: columns(a["kv_down_proj_2"], 0, P, 0, DT_)),
                                          (1, DT_, P, lambda i: columns(a["kv_down_proj_2"], P, P, 0, DT_)),
                                          (2, DT_, 64, lambda i: columns(a["kv_down_proj_2"], 2 * P, 64, 0, DT_)),
                                          (3, DT_, P, lambda i: columns(a["q_down_proj_2"][0], 0, P, 0, DT_)),
                                          (0, DT_, P, lambda i: columns(a["q_down_proj_2"][0], P, P, 0, DT_)),
                                          (1, DT_, P, lambda i: columns(a["q_down_proj_2"][0], 2 * P, P, 0, DT_))],
                           SLOTS)
            st_mla = stage("latent attention", HEADS, [
                (0, 3, 192, lambda i: columns(a["q_up_proj_2"][0], i * 192, 192, 0, 3)),
                (1, 2, P, lambda i: columns(a["kv_up_k_2"], i * P, P, 0, 2)),
                (2, 2, P, lambda i: columns(a["kv_up_v_2"], i * P, P, 0, 2))], 3)
            st_mo = square_stage("latent attention out", a["attn_out_proj_2"][0], DT_, 4, (8,))
        elif section == "ssd":
            w_in = a["ssd_in_proj_2"][0]
            st_dt = stage("step sizes", 1, [(0, DT_, SSD_H, lambda i: columns(
                w_in, 2 * SSD_INNER + 2 * GROUPS * SSD_STATE, SSD_H, 0, DT_))], 1)
            b0 = 2 * SSD_INNER
            places = ((b0, 1), (b0 + GROUPS * SSD_STATE, 1), (SSD_INNER, 2), (SSD_INNER + P, 2),
                      (0, 2), (P, 2))
            st_ssd = []
            for half in range(2):
                st_ssd.append((
                    stage("ssd", 4, [(n % 3, DT_, P, lambda i, c=c, step=step, half=half: columns(
                        w_in, address(i, step, c + 4 * half * step * P), P, 0, DT_))
                        for n, (c, step) in enumerate(places)], 3),
                    stage("ssd out", 1, [(n % 3, DT_, P, lambda i, n=n, half=half: columns(
                        a["ssd_out_proj_2"][0], n * P, P, half * 8, DT_)) for n in range(DT_)], 3)))
    uses = [0] * SLOTS
    for st in stream:
        uses = st.place(uses)
    follows = dict(zip(stream, stream[1:]))

    def first_slabs(st):
        return [(st, p, 0) for p in range(st.ahead)] if st else []

    def next_slabs(st, i):
        return [(st, p, i) for p in range(st.ahead, len(st.slabs))] + [(st, p, i + 1) for p in range(st.ahead)]

    def last_slabs(st):
        return [(st, p, st.iters - 1) for p in range(st.ahead, len(st.slabs))] + first_slabs(follows.get(st))

    def load_slabs(sp):
        for st in stream:
            with loop(sp, st.iters) as i:
                for pos, (slot, k, width, source) in enumerate(st.slabs):
                    sp.wait_ge(s.lo_done[slot], st.use(pos, i))
                    sp.dma_start(stg[:, slot, 0:k * width].rearrange("p (k c) -> p k c", k=k),
                                 source(i)).then_inc(s.landed[slot], 16)

    def split_hi(act, slab):
        st, pos, i = slab
        slot, k, width, _ = st.slabs[pos]
        act.wait_ge(s.landed[slot], st.use(pos, i) * 16)
        act.wait_ge(s.multiplied[slot], st.use(pos, i))
        act.activation(wh[:, slot, 0:k * width], stg[:, slot, 0:k * width], ACT.Copy).then_inc(s.hi_done[slot], 1)

    def split_lo(pool, slab):
        st, pos, i = slab
        slot, k, width, _ = st.slabs[pos]
        pool.wait_ge(s.hi_done[slot], st.use(pos, i))
        pool.tensor_tensor(wl[:, slot, 0:k * width], stg[:, slot, 0:k * width],
                           wh[:, slot, 0:k * width].bitcast(F32), ALU.subtract).then_inc(s.lo_done[slot], 1)

    def split_lo_stage(pool, st):
        if st.iters > 1:
            with loop(pool, st.iters - 1) as i:
                for slab in next_slabs(st, i):
                    split_lo(pool, slab)
        for slab in last_slabs(st):
            split_lo(pool, slab)

    def wait_product(eng, st, pos, i):
        eng.wait_ge(s.multiplied[st.slabs[pos][0]], st.use(pos, i) + 1)

    def product(pe, po, lh, ll, rh, rl, start, stop):
        pe.matmul(po, lh, rh, start=start, stop=False)
        pe.matmul(po, lh, rl, start=False, stop=False)
        return pe.matmul(po, ll, rh, start=False, stop=stop)

    def multiply(pe, st, pos, i, po, xh, xl, x0, col0=0, m=P, first=True, last=True, signal=True, ready=None):
        slot, k, width, _ = st.slabs[pos]
        pe.wait_ge(s.lo_done[slot], st.use(pos, i) + 1)
        for j in range(k):
            if ready:
                ready(j)
            c = j * width + col0
            end = product(pe, po, wh[:, slot, c:c + m], wl[:, slot, c:c + m], xh[:, x0 + j, :], xl[:, x0 + j, :],
                          first and j == 0, last and j == k - 1)
        if signal:
            end.then_inc(s.multiplied[slot], 1)

    acc_before = [0]

    class Dense:

        def __init__(self, st, xh, xl, parts, ready, kind):
            self.st, self.xh, self.xl, self.parts, self.ready, self.kind = st, xh, xl, parts, ready, kind
            self.tiles = len(st.slabs) // parts
            self.ring = min(self.tiles, 4)
            self.bank = 4 if parts > 1 or self.tiles > 4 else 0
            self.before = acc_before[0]
            acc_before[0] += self.tiles * st.iters

        def tensor(self, pe):
            st = self.st
            with loop(pe, st.iters) as i:
                for t in range(self.tiles):
                    pe.wait_ge(s.acc_done, self.tiles * i + (SEED + self.before + t - self.ring + 1))
                    x0 = 0
                    for q in range(self.parts):
                        pos = t * self.parts + q
                        multiply(pe, st, pos, i, ps[:, self.bank + t % self.ring, :], self.xh, self.xl, x0, first=q == 0,
                                 last=q == self.parts - 1,
                                 ready=(lambda j, x0=x0: self.ready(pe, x0 + j)) if t == 0 else None)
                        x0 += st.slabs[pos][1]

        def scalar(self, act):
            st = self.st

            def body(i, slabs):
                for slab in slabs:
                    split_hi(act, slab)
            if st.iters > 1:
                with loop(act, st.iters - 1) as i:
                    body(i, next_slabs(st, i))
            body(st.iters - 1, last_slabs(st))

        def vector(self, dve):
            st = self.st
            with loop(dve, st.iters) as i:
                for t in range(self.tiles):
                    wait_product(dve, st, (t + 1) * self.parts - 1, i)
                    m = tile(acc, self.tiles * i + t)
                    if self.kind == "copy":
                        dve.tensor_copy(m, ps[:, self.bank + t % self.ring, :]).then_inc(s.acc_done, 1)
                    else:
                        dve.tensor_tensor(m, m, ps[:, self.bank + t % self.ring, :], ALU.add).then_inc(s.acc_done, 1)

        def gpsimd(self, pool):
            split_lo_stage(pool, self.st)

        def done(self, eng, j):
            eng.wait_ge(s.acc_done, SEED + self.before + j + 1)

    tiles_before = [0]
    hidden_before = [0]

    class Up:

        def __init__(self, st, h):
            self.st, self.h, self.tiles = st, h, 4
            self.before = tiles_before[0]
            tiles_before[0] += self.tiles * st.iters
            self.hid = hidden_before[0]
            hidden_before[0] += self.tiles * st.iters
            self.sq = squares_before[0]
            squares_before[0] += self.tiles * st.iters

        def tensor(self, pe):
            with loop(pe, self.st.iters) as i:
                for t in range(4):
                    pe.wait_ge(s.bank_free, 4 * i + (SEED + self.before + t - 3))
                    multiply(pe, self.st, t, i, ps[:, t, :], hh, hl, 0,
                             ready=(lambda j: self.h.ready(pe, j)) if t == 0 else None)

        def scalar(self, act):
            def body(i, slabs):
                for t in range(4):
                    wait_product(act, self.st, t, i)
                    act.wait_ge(s.squared, 4 * i + (SEED + self.sq + t - 1))
                    act.activation(tmp[:, t % 2, :], ps[:, t, :], ACT.Relu).then_inc(s.bank_free, 1)
                    if t < len(slabs):
                        split_hi(act, slabs[t])
                    act.wait_ge(s.squared, 4 * i + (SEED + self.sq + t + 1))
                    act.activation(tile(bh, 4 * i + t), tmp[:, 2 + t % 2, :], ACT.Copy).then_inc(s.hid_hi, 1)
                for slab in slabs[4:]:
                    split_hi(act, slab)
            with loop(act, self.st.iters - 1) as i:
                body(i, next_slabs(self.st, i))
            body(self.st.iters - 1, last_slabs(self.st))

        def vector(self, dve):
            with loop(dve, self.st.iters) as i:
                for t in range(4):
                    dve.wait_ge(s.bank_free, 4 * i + (SEED + self.before + t + 1))
                    dve.tensor_tensor(tmp[:, 2 + t % 2, :], tmp[:, t % 2, :], tmp[:, t % 2, :],
                                      ALU.mult).then_inc(s.squared, 1)
                    dve.wait_ge(s.hid_hi, 4 * i + (self.hid + t + 1))
                    dve.tensor_tensor(tile(bl, 4 * i + t), tmp[:, 2 + t % 2, :],
                                      tile(bh, 4 * i + t).bitcast(F32), ALU.subtract).then_inc(s.hid_lo, 1)

        def gpsimd(self, pool):
            split_lo_stage(pool, self.st)

    squares_before = [0]

    def hidden_ready(before):
        return lambda pe, k: pe.wait_ge(s.hid_lo, before + k + 1)


    class Reduction:
        count = 0
        stats = 0
        pows = 0

        def __init__(self, n, width, eps, bank, squares=True):
            self.n, self.scale, self.eps, self.bank, self.squares = n, 1.0 / width, eps, bank, squares
            self.r, self.s0, self.p = Reduction.count, Reduction.stats, Reduction.pows
            self.q0 = Reduction.sq
            Reduction.count += 1
            Reduction.stats += n
            Reduction.pows += squares
            Reduction.sq += n * squares

        sq = 0

        def square(self, act, j, src):
            if self.squares:
                act.wait_ge(s.stat_used, SEED + self.s0 + j - 1)
                act.activation(tmp[:, 4 + j % 2, :], src, ACT.Square).then_inc(s.stat_in, 1)

        def tensor(self, pe, src=None, ready=None):
            for j in range(self.n):
                if self.squares:
                    pe.wait_ge(s.stat_in, self.q0 + j + 1)
                    src_j = tmp[:, 4 + j % 2, :]
                else:
                    ready(pe, j)
                    src_j = src(j)
                for b in range(TB):
                    end = pe.matmul(ps[:, 7, b:b + 1], src_j[:, b * P:(b + 1) * P], ones[:, 0:1],
                                    start=j == 0 and b == 0, stop=j == self.n - 1, skip_group_check=True)
                end.then_inc(s.stat_used, 1)
            pe.wait_ge(s.diag_done, self.r + 1)
            pe.matmul(ps[:, self.bank, :], ones, diag[:], start=True, stop=True).then_inc(s.bc_done, 1)

        def vector(self, dve):
            dve.wait_ge(s.stat_used, SEED + self.s0 + self.n)
            dve.tensor_scalar(stat4, ps[:, 7, 0:4], self.scale, self.eps, ALU.mult, ALU.add).then_inc(s.var_done, 1)
            if self.squares:
                dve.wait_ge(s.rstd_done, self.p + 1)
                r = rstd4
            else:
                dve.wait_ge(s.var_done, self.r + 1)
                r = stat4
            dve.wait_ge(s.bc_done, self.r)
            dve.tensor_tensor(diag[:].rearrange("p (b t) -> p b t", b=TB),
                              ident.rearrange("p (a t) -> p a t", a=1).to_broadcast([P, TB, P]),
                              r.rearrange("p (b a) -> p b a", a=1).to_broadcast([P, TB, P]),
                              ALU.mult).then_inc(s.diag_done, 1)

        def gpsimd(self, pool):
            if self.squares:
                pool.wait_ge(s.var_done, self.r + 1)
                pool.tensor_tensor(rstd4, stat4, half4, ALU.pow).then_inc(s.rstd_done, 1)

        def ready(self, eng):
            eng.wait_ge(s.bc_done, self.r + 1)

    tallies = {}

    def tally(name, n):
        tallies[name] = tallies.get(name, 0) + n
        return tallies[name] - n

    class PreNorm:

        def __init__(self, gain, layer, waits):
            self.gain, self.layer, self.waits = gain, layer, waits
            self.red = Reduction(DT_, D, EPS, 4)
            self.h = tally("h", DT_)

        def scalar(self, act):
            for j in range(DT_):
                self.waits(act, j)
                self.red.square(act, j, xT[:, j, :])
            for j in range(DT_):
                act.wait_ge(s.h_new, self.h + j + 1)
                act.activation(hh[:, j, :], acc[:, j, :], ACT.Copy).then_inc(s.h_hi, 1)

        def tensor(self, pe):
            self.red.tensor(pe)

        def vector(self, dve):
            self.red.vector(dve)
            self.red.ready(dve)

            def low(j):
                dve.wait_ge(s.h_hi, self.h + j + 1)
                dve.tensor_tensor(hl[:, j, :], acc[:, j, :], hh[:, j, :].bitcast(F32),
                                  ALU.subtract).then_inc(s.h_lo, 1)
            for j in range(DT_):
                self.waits(dve, j)
                dve.scalar_tensor_tensor(acc[:, j, :], xT[:, j, :], v(self.gain, self.layer * DT_ + j),
                                         ps[:, 4, :], ALU.mult, ALU.mult).then_inc(s.h_new, 1)
                if j > 0:
                    low(j - 1)
            low(DT_ - 1)

        def gpsimd(self, pool):
            self.red.gpsimd(pool)

        def ready(self, pe, k):
            pe.wait_ge(s.h_lo, self.h + k + 1)

    class PostNorm:

        def __init__(self, gain, layer, dense):
            self.gain, self.layer, self.dense = gain, layer, dense
            self.red = Reduction(DT_, D, EPS, 6)
            self.n = tally("norm", DT_)
            self.x = tally("x", DT_)

        def scalar(self, act):
            for j in range(DT_):
                self.dense.done(act, j)
                self.red.square(act, j, acc[:, j, :])

        def tensor(self, pe):
            self.red.tensor(pe)

        def vector(self, dve):
            self.red.vector(dve)
            self.red.ready(dve)

            def add(j):
                dve.wait_ge(s.normed, self.n + j + 1)
                dve.tensor_tensor(xT[:, j, :], xT[:, j, :], acc[:, j, :], ALU.add).then_inc(s.x_new, 1)
            for j in range(DT_):
                dve.scalar_tensor_tensor(acc[:, j, :], acc[:, j, :], v(self.gain, self.layer * DT_ + j),
                                         ps[:, 6, :], ALU.mult, ALU.mult).then_inc(s.normed, 1)
                if j > 0:
                    add(j - 1)
            add(DT_ - 1)

        def gpsimd(self, pool):
            self.red.gpsimd(pool)

        def done(self, eng, j):
            eng.wait_ge(s.x_new, self.x + j + 1)

    ORDER = (3, 2, 0, 1)
    SCORED = {3: (1, 2), 2: (6, 6), 0: (6, 6), 1: (8, 8)}
    MAXED = {3: 1, 2: 3, 0: 3, 1: 4}
    SCORE = {(c, 3): (c, 0) for c in range(2)} | {(c, 2): (2 + c, 0) for c in range(2)}
    SCORE |= {(c, 0): (2 + c, 384) for c in range(2)} | {(c, 1): (4, 256 * c) for c in range(2)}
    POFF = {0: 0, 1: 128, 2: 384, 3: 768}

    def attended(eng_transpose, src, done):
        for kt in (0, 1, 3, 2):
            bank, off = TRI[kt]
            for b in range(kt, TB):
                end = eng_transpose(ps[:, bank, off + (b - kt) * P:off + (b - kt + 1) * P],
                                    src[:, POFF[b] + kt * P:POFF[b] + (kt + 1) * P], ident)
            if kt != 1:
                end.then_inc(done, 1)

    class DiffAttention:
        V_, Q_, K_, A_ = 8, 9, 10, 11
        cos, sin = cb[:, 0, :], cb[:, 1, :]
        prob = [acc[:, 2:5, :].rearrange("p a t -> p (a t)"), acc[:, 5:8, :].rearrange("p a t -> p (a t)")]

        def __init__(self, st, h):
            self.st, self.h = st, h

        def project(self, pe, h):
            for c in range(3):
                multiply(pe, self.st, c, h, ps[:, 5 + c, :], hh, hl, 0,
                         ready=(lambda j: self.h.ready(pe, j)) if c == 0 else None)

        def scores(self, pe, h):
            pe.wait_ge(s.qk_lo, 2 * h + 2)
            pe.wait_ge(s.v_lo, h + 1)
            pe.wait_ge(s.ot_lo, h + SEED)
            for b in ORDER:
                for c in range(2):
                    bank, off = SCORE[c, b]
                    n, q0 = (b + 1) * P, b * P
                    rows = slice(64 * c, 64 * c + 64)
                    if (c, b) == (1, 1):
                        pe.wait_ge(s.scores_done, 8 * h + 2 * ORDER.index(b) + 1)
                    product(pe, ps[:, bank, off:off + n],
                            bh[rows, self.Q_, q0:q0 + P], bl[rows, self.Q_, q0:q0 + P],
                            bh[rows, self.K_, 0:n], bl[rows, self.K_, 0:n], True, False)
                    pe.matmul(ps[:, bank, off + n - P:off + n], ident_r, mask_r,
                              start=False, stop=True).then_inc(s.scores_done, 1)

        def values(self, pe, h):
            pe.wait_ge(s.combined, 4 * h + 4)
            attended(pe.transpose, self.prob[0], s.at_done)
            pe.wait_ge(s.at_lo, 3 * h + 3)
            for b in range(TB):
                for kt in range(b + 1):
                    t, off = TRI[kt]
                    w = slice(off + (b - kt) * P, off + (b - kt + 1) * P)
                    k = slice(kt * P, (kt + 1) * P)
                    end = product(pe, ps[:, 3, b * P:(b + 1) * P], bh[:, self.A_ + t, w], bl[:, self.A_ + t, w],
                                  bh[:, self.V_, k], bl[:, self.V_, k], kt == 0, kt == b)
            end.then_inc(s.pv_done, 1)

        def turn(self, pe, h):
            for c in range(2):
                pe.wait_ge(s.raw_done, 3 * h + c + 1)
                pe.matmul(ps[:, 5 + c, :], rot, tmp[:, c, :], start=True, stop=True).then_inc(s.rot_done, 1)
            pe.wait_ge(s.raw_done, 3 * h + 3)
            for b in range(TB):
                end = pe.transpose(ps[:, 7, b * P:(b + 1) * P], tmp[:, 2, b * P:(b + 1) * P], ident)
            end.then_inc(s.vt_done, 1)

        def out_transposed(self, pe, h):
            pe.wait_ge(s.o_norm, h + 1)
            for b in range(TB):
                end = pe.transpose(ps[:, 4, b * P:(b + 1) * P], tmp[:, 5, b * P:(b + 1) * P], ident)
            end.then_inc(s.ot_done, 1)

        def tensor(self, pe):
            self.project(pe, 0)
            self.turn(pe, 0)
            with loop(pe, HEADS - 1) as h:
                self.scores(pe, h)
                self.project(pe, h + 1)
                self.values(pe, h)
                self.turn(pe, h + 1)
                self.out_transposed(pe, h)
            self.scores(pe, HEADS - 1)
            self.values(pe, HEADS - 1)
            self.out_transposed(pe, HEADS - 1)

        def exps(self, act, h):
            for n, b in enumerate(ORDER):
                act.wait_ge(s.negmax, 4 * h + MAXED[b])
                for c in range(2):
                    bank, off = SCORE[c, b]
                    w = (b + 1) * P
                    act.activation(self.prob[c][:, POFF[b]:POFF[b] + w], ps[:, bank, off:off + w], ACT.Exp,
                                   bias=nm[:, 2 * n + c:2 * n + c + 1], scale=64 ** -0.5,
                                   accum_out=den[:, 2 * n + c:2 * n + c + 1]).then_inc(s.exp_done, 1)

        def raws(self, act, h, slabs):
            for c in range(3):
                wait_product(act, self.st, c, h)
                act.activation(tmp[:, c, :], ps[:, 5 + c, :], ACT.Copy).then_inc(s.raw_done, 1)
                if c < len(slabs):
                    split_hi(act, slabs[c])
            for slab in slabs[3:]:
                split_hi(act, slab)

        def probs_hi(self, act, h):
            for b in range(3):
                act.wait_ge(s.at_done, 3 * h + b + 1)
                act.activation(bh[:, self.A_ + b, 0:TRI_W[b]], ps[:, b, 0:TRI_W[b]], ACT.Copy).then_inc(s.at_hi, 1)
            act.wait_ge(s.pv_done, h + 1)
            for b in range(TB):
                act.activation(tmp[:, 5, b * P:(b + 1) * P], ps[:, 3, b * P:(b + 1) * P], ACT.Square,
                               accum_out=oss[:, b:b + 1]).then_inc(s.o_sq, 1)

        def qkv_hi(self, act, h):
            for c, t in enumerate((self.Q_, self.K_)):
                act.wait_ge(s.rope_done, 6 * h + 3 * c + 3)
                act.activation(bh[:, t, :], tmp[:, c, :], ACT.Copy).then_inc(s.qk_hi, 1)
            act.wait_ge(s.vt_done, h + 1)
            act.activation(bh[:, self.V_, :], ps[:, 7, :], ACT.Copy).then_inc(s.v_hi, 1)

        def out_hi(self, act, h):
            act.wait_ge(s.ot_done, h + 1)
            act.activation(tile(bh, h), ps[:, 4, :], ACT.Copy, scale=subg).then_inc(s.ot_hi, 1)

        def scalar(self, act):
            self.raws(act, 0, next_slabs(self.st, 0))
            self.qkv_hi(act, 0)

            def body(h, slabs):
                self.exps(act, h)
                self.raws(act, h + 1, slabs)
                self.probs_hi(act, h)
                self.qkv_hi(act, h + 1)
                self.out_hi(act, h)
            with loop(act, HEADS - 2) as h:
                body(h, next_slabs(self.st, h + 1))
            body(HEADS - 2, last_slabs(self.st))
            self.exps(act, HEADS - 1)
            self.probs_hi(act, HEADS - 1)
            self.out_hi(act, HEADS - 1)

        def softmax(self, dve, h):
            for n, b in enumerate(ORDER):
                for c in range(2):
                    bank, off = SCORE[c, b]
                    dve.wait_ge(s.scores_done, 8 * h + SCORED[b][c])
                    dve.reduce_max(mx[:, 2 * n + c:2 * n + c + 1], ps[:, bank, off:off + (b + 1) * P],
                                   axis=AX_X).then_inc(s.max_done, 1)
                dve.wait_ge(s.max_done, 8 * h + 2 * n + 2)
                dve.tensor_scalar(nm[:, 2 * n:2 * n + 2], mx[:, 2 * n:2 * n + 2], -(64 ** -0.5), None,
                                  ALU.mult).then_inc(s.negmax, 1)
            for n, b in enumerate(ORDER):
                r = slice(POFF[b], POFF[b] + (b + 1) * P)
                i0, i1 = inv[:, 2 * n:2 * n + 1], inv[:, 2 * n + 1:2 * n + 2]
                dve.wait_ge(s.exp_done, 8 * h + 2 * n + 2)
                dve.reciprocal(inv[:, 2 * n:2 * n + 2], den[:, 2 * n:2 * n + 2]).then_inc(s.inv_done, 1)
                dve.wait_ge(s.inv_done, 8 * h + 2 * n + 1)
                dve.tensor_scalar(i1, i1, lam, None, ALU.mult).then_inc(s.inv_done, 1)
                dve.wait_ge(s.inv_done, 8 * h + 2 * n + 2)
                dve.tensor_scalar(self.prob[1][:, r], self.prob[1][:, r], i1, None, ALU.mult).then_inc(s.weighed, 1)
                dve.wait_ge(s.weighed, 4 * h + n + 1)
                dve.scalar_tensor_tensor(self.prob[0][:, r], self.prob[0][:, r], i0, self.prob[1][:, r],
                                         ALU.mult, ALU.add).then_inc(s.combined, 1)

        def probs_lo(self, dve, h):
            for b in range(3):
                dve.wait_ge(s.at_hi, 3 * h + b + 1)
                w = slice(0, TRI_W[b])
                dve.tensor_tensor(bl[:, self.A_ + b, w], ps[:, b, w], bh[:, self.A_ + b, w].bitcast(F32),
                                  ALU.subtract).then_inc(s.at_lo, 1)
            dve.wait_ge(s.o_sq, 4 * h + 4)
            dve.tensor_scalar(ovar, oss, 1.0 / P, EPS, ALU.mult, ALU.add).then_inc(s.o_var, 1)

        def rope(self, dve, h, c):
            dve.wait_ge(s.rot_done, 2 * h + c + 1)
            dve.tensor_tensor(tmp[:, 3 + c, :], ps[:, 5 + c, :], self.sin, ALU.mult).then_inc(s.rope_done, 1)
            dve.tensor_tensor(tmp[:, c, :], tmp[:, c, :], self.cos, ALU.mult).then_inc(s.rope_done, 1)
            dve.wait_ge(s.rope_done, 6 * h + 3 * c + 2)
            dve.tensor_tensor(tmp[:, c, :], tmp[:, c, :], tmp[:, 3 + c, :], ALU.add).then_inc(s.rope_done, 1)

        def out_norm(self, dve, h):
            dve.wait_ge(s.o_rstd, h + 1)
            dve.tensor_tensor(tmp[:, 5, :].rearrange("p (b e) -> p b e", b=TB),
                              ps[:, 3, :].rearrange("p (b e) -> p b e", b=TB),
                              orstd.rearrange("p (b a) -> p b a", a=1).to_broadcast([P, TB, P]),
                              ALU.mult).then_inc(s.o_norm, 1)

        def qkv_lo(self, dve, h):
            for c, t in enumerate((self.Q_, self.K_)):
                dve.wait_ge(s.qk_hi, 2 * h + c + 1)
                dve.tensor_tensor(bl[:, t, :], tmp[:, c, :], bh[:, t, :].bitcast(F32),
                                  ALU.subtract).then_inc(s.qk_lo, 1)
            dve.wait_ge(s.v_hi, h + 1)
            dve.tensor_tensor(bl[:, self.V_, :], ps[:, 7, :], bh[:, self.V_, :].bitcast(F32),
                              ALU.subtract).then_inc(s.v_lo, 1)

        def out_lo(self, dve, h):
            dve.wait_ge(s.ot_hi, h + 1)
            dve.scalar_tensor_tensor(tile(bl, h), ps[:, 4, :], subg, tile(bh, h).bitcast(F32),
                                     ALU.mult, ALU.subtract).then_inc(s.ot_lo, 1)

        def vector(self, dve):
            self.rope(dve, 0, 0)
            self.rope(dve, 0, 1)
            self.qkv_lo(dve, 0)
            with loop(dve, HEADS - 1) as h:
                self.softmax(dve, h)
                self.probs_lo(dve, h)
                self.rope(dve, h + 1, 0)
                self.out_norm(dve, h)
                self.rope(dve, h + 1, 1)
                self.qkv_lo(dve, h + 1)
                self.out_lo(dve, h)
            self.softmax(dve, HEADS - 1)
            self.probs_lo(dve, HEADS - 1)
            self.out_norm(dve, HEADS - 1)
            self.out_lo(dve, HEADS - 1)

        def gpsimd(self, pool):
            for slab in next_slabs(self.st, 0):
                split_lo(pool, slab)

            def body(h, slabs):
                for slab in slabs:
                    split_lo(pool, slab)
                pool.wait_ge(s.o_var, h + 1)
                pool.tensor_tensor(orstd, ovar, half4, ALU.pow).then_inc(s.o_rstd, 1)
            with loop(pool, HEADS - 2) as h:
                body(h, next_slabs(self.st, h + 1))
            body(HEADS - 2, last_slabs(self.st))
            body(HEADS - 1, [])

        def ready(self, pe, k):
            pe.wait_ge(s.ot_lo, SEED + k + 1)

    class ShortConv:
        def __init__(self, st, h):
            self.st, self.h = st, h
            self.hid = hidden_before[0]
            hidden_before[0] += DT_

        def tensor(self, pe):
            with loop(pe, 4) as i:
                for u in range(2):
                    for n, read in enumerate((s.c_copied, s.conv_u, s.gated)):
                        pe.wait_ge(read, 2 * i + (SEED + u - 1))
                        multiply(pe, self.st, 3 * u + n, i, ps[:, 3 * u + n, :], hh, hl, 0,
                                 ready=(lambda j: self.h.ready(pe, j)) if u == 0 and n == 0 else None)

        def scalar(self, act):
            def body(i, slabs):
                for u in range(2):
                    wait_product(act, self.st, 3 * u, i)
                    act.wait_ge(s.hid_lo, 2 * i + (self.hid + u - 1))
                    act.activation(tmp[:, 3 * u, :], ps[:, 3 * u, :], ACT.Copy).then_inc(s.c_copied, 1)
                    split_hi(act, slabs[3 * u])
                    act.wait_ge(s.conv_u, 2 * i + (SEED + u + 1))
                    act.activation(tmp[:, 3 * u + 2, :], tmp[:, 3 * u + 1, :], ACT.Copy,
                                   scale=v("conv_w", 16 + 2 * i + u)).then_inc(s.conv_scaled, 1)
                    split_hi(act, slabs[3 * u + 1])
                    if 3 * u + 2 < len(slabs):
                        split_hi(act, slabs[3 * u + 2])
                    act.wait_ge(s.gated, 2 * i + (SEED + u + 1))
                    act.activation(tile(bh, 2 * i + u), tmp[:, 3 * u, :], ACT.Copy).then_inc(s.hid_hi, 1)
                for slab in slabs[6:]:
                    split_hi(act, slab)
            with loop(act, 3) as i:
                body(i, next_slabs(self.st, i))
            body(3, last_slabs(self.st))

        def vector(self, dve):
            with loop(dve, 4) as i:
                for u in range(2):
                    t0, t1, t2 = (tmp[:, 3 * u + n, :] for n in range(3))
                    wait_product(dve, self.st, 3 * u + 1, i)
                    dve.wait_ge(s.c_copied, 2 * i + (SEED + u + 1))
                    dve.tensor_tensor(t1, t0, ps[:, 3 * u + 1, :], ALU.mult).then_inc(s.conv_u, 1)
                    dve.wait_ge(s.conv_scaled, 2 * i + u + 1)
                    dve.scalar_tensor_tensor(t2[:, 1:T], t1[:, 0:T - 1], v("conv_w", 8 + 2 * i + u), t2[:, 1:T],
                                             ALU.mult, ALU.add).then_inc(s.conv_tap, 1)
                    dve.wait_ge(s.conv_tap, 4 * i + 2 * u + 1)
                    dve.scalar_tensor_tensor(t2[:, 2:T], t1[:, 0:T - 2], v("conv_w", 2 * i + u), t2[:, 2:T],
                                             ALU.mult, ALU.add).then_inc(s.conv_tap, 1)
                    dve.wait_ge(s.conv_tap, 4 * i + 2 * u + 2)
                    wait_product(dve, self.st, 3 * u + 2, i)
                    dve.tensor_tensor(t0, ps[:, 3 * u + 2, :], t2, ALU.mult).then_inc(s.gated, 1)
                    dve.wait_ge(s.hid_hi, 2 * i + (self.hid + u + 1))
                    dve.tensor_tensor(tile(bl, 2 * i + u), t0, tile(bh, 2 * i + u).bitcast(F32),
                                      ALU.subtract).then_inc(s.hid_lo, 1)

        def gpsimd(self, pool):
            split_lo_stage(pool, self.st)

    class SplitX:

        def __init__(self, waits):
            self.waits, self.h = waits, tally("h", DT_)

        def scalar(self, act):
            for j in range(DT_):
                self.waits(act, j)
                act.activation(hh[:, j, :], xT[:, j, :], ACT.Copy).then_inc(s.h_hi, 1)

        def vector(self, dve):
            for j in range(DT_):
                dve.wait_ge(s.h_hi, self.h + j + 1)
                dve.tensor_tensor(hl[:, j, :], xT[:, j, :], hh[:, j, :].bitcast(F32), ALU.subtract).then_inc(s.h_lo, 1)

        def tensor(self, pe):
            pass

        gpsimd = tensor

        def ready(self, pe, k):
            pe.wait_ge(s.h_lo, self.h + k + 1)

    class LayerNorm:

        def __init__(self, gain, bias, layer, dense, from_parts=False, last=False):
            self.gain, self.bias, self.layer, self.dense = gain, bias, layer, dense
            self.from_parts, self.last = from_parts, last
            self.mean = Reduction(DT_, D, 0.0, 5, squares=False)
            self.var = Reduction(DT_, D, LN_EPS, 6)
            self.sum = tally("ln_sum", DT_ * (1 + from_parts))
            self.cen, self.n, self.x = tally("centered", DT_), tally("norm", DT_), tally("ln_x", DT_)
            self.h = 0 if last else tally("h", DT_)

        def summed(self, eng, j):
            eng.wait_ge(s.ln_sum, self.sum + (j + 1) * (1 + self.from_parts))

        def tensor(self, pe):
            self.mean.tensor(pe, src=lambda j: acc[:, j, :], ready=self.summed)
            self.var.tensor(pe)

        def scalar(self, act):
            for j in range(DT_):
                act.wait_ge(s.centered, self.cen + j + 1)
                self.var.square(act, j, acc[:, j, :])
            for j in range(DT_):
                act.wait_ge(s.normed, self.n + j + 1)
                b = v(self.bias, self.layer * DT_ + j)
                act.activation(xT[:, j, :], acc[:, j, :], ACT.Identity, bias=b).then_inc(s.ln_x, 1)
                if not self.last:
                    act.activation(hh[:, j, :], acc[:, j, :], ACT.Identity, bias=b).then_inc(s.h_hi, 1)

        def vector(self, dve):
            for j in range(DT_):
                self.dense.done(dve, j)
                if self.from_parts:
                    dve.scalar_tensor_tensor(acc[:, j, :], hh[:, j, :].bitcast(F32), DN_ALPHA, acc[:, j, :],
                                             ALU.mult, ALU.add).then_inc(s.ln_sum, 1)
                    dve.wait_ge(s.ln_sum, self.sum + 2 * j + 1)
                    dve.scalar_tensor_tensor(acc[:, j, :], hl[:, j, :].bitcast(F32), DN_ALPHA, acc[:, j, :],
                                             ALU.mult, ALU.add).then_inc(s.ln_sum, 1)
                else:
                    dve.scalar_tensor_tensor(acc[:, j, :], xT[:, j, :], DN_ALPHA, acc[:, j, :],
                                             ALU.mult, ALU.add).then_inc(s.ln_sum, 1)
            self.mean.vector(dve)
            self.mean.ready(dve)
            for j in range(DT_):
                dve.tensor_tensor(acc[:, j, :], acc[:, j, :], ps[:, 5, :], ALU.subtract).then_inc(s.centered, 1)
            self.var.vector(dve)
            self.var.ready(dve)

            def low(j):
                dve.wait_ge(s.h_hi, self.h + j + 1)
                dve.tensor_tensor(hl[:, j, :], xT[:, j, :], hh[:, j, :].bitcast(F32), ALU.subtract).then_inc(s.h_lo, 1)
            for j in range(DT_):
                dve.scalar_tensor_tensor(acc[:, j, :], acc[:, j, :], v(self.gain, self.layer * DT_ + j),
                                         ps[:, 6, :], ALU.mult, ALU.mult).then_inc(s.normed, 1)
                if j > 0 and not self.last:
                    low(j - 1)
            if not self.last:
                low(DT_ - 1)

        def gpsimd(self, pool):
            self.mean.gpsimd(pool)
            self.var.gpsimd(pool)

        def done(self, eng, j):
            eng.wait_ge(s.ln_x, self.x + j + 1)

        def ready(self, pe, k):
            pe.wait_ge(s.h_lo, self.h + k + 1)

    class GatedUp:

        def __init__(self, st, layer, tile0, h):
            self.st, self.w0, self.b0, self.h = st, layer * 3 * 2 * FFN_T + tile0, layer * 2 * FFN_T + tile0, h
            self.before = tally("ffn_bank", 4 * st.iters)
            self.n = tally("ffn_tiles", 2 * st.iters)
            self.hid = hidden_before[0]
            hidden_before[0] += 2 * st.iters

        def taps(self, n, tap, i, u):
            return v("ffn_w", 2 * i + (self.w0 + tap * 2 * FFN_T + n * FFN_T + u))

        def tensor(self, pe):
            with loop(pe, self.st.iters) as i:
                for t in range(4):
                    pe.wait_ge(s.conv_read, 4 * i + (SEED + self.before + t - 3))
                    multiply(pe, self.st, t, i, ps[:, t, :], hh, hl, 0,
                             ready=(lambda j: self.h.ready(pe, j)) if t == 0 else None)

        def scalar(self, act):
            def body(i, slabs):
                for u in range(2):
                    act.wait_ge(s.hid_lo, 2 * i + (self.hid + u - 1))
                    for n in range(2):
                        wait_product(act, self.st, 2 * u + n, i)
                        act.activation(tmp[:, 3 * u + n, :], ps[:, 2 * u + n, :], ACT.Identity,
                                       bias=v("ffn_b", 2 * i + (self.b0 + n * FFN_T + u)),
                                       scale=self.taps(n, 2, i, u)).then_inc(s.ffn_scaled, 1)
                        if 2 * u + n < len(slabs):
                            split_hi(act, slabs[2 * u + n])
                    act.wait_ge(s.conv_read, 4 * i + (SEED + self.before + 2 * u + 1))
                    act.activation(tmp[:, 3 * u + 2, :], tmp[:, 3 * u, :], ACT.Tanh, scale=0.5).then_inc(s.ffn_gate, 1)
                    act.wait_ge(s.ffn_hidden, 2 * i + (self.n + u + 1))
                    act.activation(tile(bh, 2 * i + u), tmp[:, 3 * u + 1, :], ACT.Copy).then_inc(s.hid_hi, 1)
                for slab in slabs[4:]:
                    split_hi(act, slab)
            with loop(act, self.st.iters - 1) as i:
                body(i, next_slabs(self.st, i))
            body(self.st.iters - 1, last_slabs(self.st))

        def vector(self, dve):
            with loop(dve, self.st.iters) as i:
                for u in range(2):
                    for n in range(2):
                        x, y = ps[:, 2 * u + n, :], tmp[:, 3 * u + n, :]
                        dve.wait_ge(s.ffn_scaled, 4 * i + (2 * self.n + 2 * u + n + 1))
                        dve.scalar_tensor_tensor(y[:, 1:T], x[:, 0:T - 1], self.taps(n, 1, i, u), y[:, 1:T],
                                                 ALU.mult, ALU.add).then_inc(s.ffn_tap, 1)
                        dve.wait_ge(s.ffn_tap, 4 * i + (2 * self.n + 2 * u + n + 1))
                        dve.scalar_tensor_tensor(y[:, 2:T], x[:, 0:T - 2], self.taps(n, 0, i, u), y[:, 2:T],
                                                 ALU.mult, ALU.add).then_inc(s.conv_read, 1)
                    gate, value, th = (tmp[:, 3 * u + n, :] for n in range(3))
                    dve.wait_ge(s.ffn_gate, 2 * i + (self.n + u + 1))
                    dve.scalar_tensor_tensor(gate, th, 1.0, gate, ALU.add, ALU.mult).then_inc(s.ffn_silu, 1)
                    dve.wait_ge(s.ffn_silu, 2 * i + (self.n + u + 1))
                    dve.scalar_tensor_tensor(value, gate, 0.5, value, ALU.mult, ALU.mult).then_inc(s.ffn_hidden, 1)
                    dve.wait_ge(s.hid_hi, 2 * i + (self.hid + u + 1))
                    dve.tensor_tensor(tile(bl, 2 * i + u), value, tile(bh, 2 * i + u).bitcast(F32),
                                      ALU.subtract).then_inc(s.hid_lo, 1)

        def gpsimd(self, pool):
            split_lo_stage(pool, self.st)

    class Latents:
        cos, sin = acc[0:64, 6, :], acc[0:64, 7, :]
        TILES = (0, 1, 3, 4, 5)
        PUT = (0, 1, 2, 3, 4)

        def __init__(self, st, h):
            self.st, self.h = st, h
            self.kv = Reduction(2, KV_RANK, EPS, 6)
            self.q = Reduction(3, Q_RANK, EPS, 6)

        def tensor(self, pe):
            for pos in range(6):
                m = MLA_ROPE if pos == 2 else P
                multiply(pe, self.st, pos, 0, ps[0:m, pos, :], hh, hl, 0, m=m,
                         ready=(lambda j: self.h.ready(pe, j)) if pos == 0 else None)
            pe.wait_ge(s.kvq_copied, 4)
            pe.matmul(ps[:, 3, :], rot2[0:64, :], acc[0:64, 2, :], start=True, stop=True).then_inc(s.kr_rot, 1)
            self.kv.tensor(pe)
            self.q.tensor(pe)

        def scalar(self, act):
            slabs = last_slabs(self.st)
            for slab in slabs[:2]:
                split_hi(act, slab)
            for j in range(2):
                act.wait_ge(s.kvq_copied, j + 1)
                self.kv.square(act, j, acc[:, j, :])
            for n, table in enumerate((self.sin, self.cos)):
                act.wait_ge(s.ang_done, 2 + 7 * (n + 1))
                act.activation(table, tmp[0:64, 2 + n, :], ACT.Sin).then_inc(s.tab_done, 1)
            for j in range(3):
                act.wait_ge(s.kvq_copied, 4 + j)
                self.q.square(act, j, acc[:, 3 + j, :])
            wait_product(act, self.st, 5, 0)
            for n, (t, put) in enumerate(zip(self.TILES, self.PUT)):
                act.wait_ge(s.kvq_norm, n + 1)
                act.activation(hh[:, put, :], acc[:, t, :], ACT.Copy).then_inc(s.kvq_hi, 1)
            act.wait_ge(s.kr_done, 3)
            act.activation(hh[0:64, 5, :], acc[0:64, 2, :], ACT.Copy).then_inc(s.kvq_hi, 1)
            for slab in slabs[2:]:
                split_hi(act, slab)

        def vector(self, dve):
            n = [0]

            def link(instruction):
                n[0] += 1
                instruction.then_inc(s.ang_done, 1)
                dve.wait_ge(s.ang_done, n[0])
            ang, k = tmp[0:64, 0, :], tmp[0:64, 1, :]
            link(dve.tensor_copy(ang, positions[:]))
            link(dve.tensor_scalar(ang, ang, v("inv_freq")[0:64], None, ALU.mult))
            for fn in range(2):
                r = tmp[0:64, 2 + fn, :]
                link(dve.tensor_scalar(k, ang, 1.0 / (2 * math.pi), 0.25 * fn, ALU.mult, ALU.add))
                link(dve.tensor_scalar(k, k, ROUND, ROUND, ALU.add, ALU.subtract))
                link(dve.scalar_tensor_tensor(r, k, -TWO_PI[0], ang, ALU.mult, ALU.add))
                link(dve.scalar_tensor_tensor(r, k, -TWO_PI[1], r, ALU.mult, ALU.add))
                link(dve.scalar_tensor_tensor(r, k, -TWO_PI[2], r, ALU.mult, ALU.add))
                link(dve.tensor_scalar(r, r, 0.5 * math.pi * fn, PI_DOWN, ALU.add, ALU.min))
                link(dve.tensor_scalar(r, r, -PI_DOWN, None, ALU.max))
            for pos in range(6):
                m = MLA_ROPE if pos == 2 else P
                wait_product(dve, self.st, pos, 0)
                dve.tensor_copy(acc[0:m, pos, :], ps[0:m, pos, :]).then_inc(s.kvq_copied, 1)
            dve.wait_ge(s.tab_done, 2)
            dve.wait_ge(s.kr_rot, 1)
            dve.tensor_tensor(tmp[0:64, 0, :], ps[0:64, 3, :], self.sin, ALU.mult).then_inc(s.kr_done, 1)
            dve.tensor_tensor(acc[0:64, 2, :], acc[0:64, 2, :], self.cos, ALU.mult).then_inc(s.kr_done, 1)
            dve.wait_ge(s.kr_done, 2)
            dve.tensor_tensor(acc[0:64, 2, :], acc[0:64, 2, :], tmp[0:64, 0, :], ALU.add).then_inc(s.kr_done, 1)
            at = 0
            for red, gain, count in ((self.kv, "kv_g", 2), (self.q, "q_g", 3)):
                red.vector(dve)
                red.ready(dve)
                for j in range(count):
                    t = acc[:, self.TILES[at], :]
                    dve.scalar_tensor_tensor(t, t, v(gain, j), ps[:, 6, :], ALU.mult, ALU.mult)\
                        .then_inc(s.kvq_norm, 1)
                    at += 1
            for n, (t, put) in enumerate(zip(self.TILES, self.PUT)):
                dve.wait_ge(s.kvq_hi, n + 1)
                dve.tensor_tensor(hl[:, put, :], acc[:, t, :], hh[:, put, :].bitcast(F32),
                                  ALU.subtract).then_inc(s.kvq_lo, 1)
            dve.wait_ge(s.kvq_hi, 6)
            dve.tensor_tensor(hl[0:64, 5, :], acc[0:64, 2, :], hh[0:64, 5, :].bitcast(F32),
                              ALU.subtract).then_inc(s.kvq_lo, 1)

        def gpsimd(self, pool):
            slabs = last_slabs(self.st)
            for slab in slabs[:2]:
                split_lo(pool, slab)
            self.kv.gpsimd(pool)
            self.q.gpsimd(pool)
            for slab in slabs[2:]:
                split_lo(pool, slab)

    class LatentAttention:
        QN, QR, KN, V_, A_ = 8, 9, 10, 11, 12
        WHERE = {3: (0, 0), 2: (1, 0), 0: (1, 384), 1: (2, 0)}
        SCORED = {3: 1, 2: 3, 0: 3, 1: 4}
        prob = acc[:, 0:3, :].rearrange("p a t -> p (a t)")
        scale = (MLA_NOPE + MLA_ROPE) ** -0.5

        def __init__(self, st):
            self.st = st

        def project(self, pe, h):
            multiply(pe, self.st, 0, h, ps[:, 5, :], hh, hl, 2, signal=False)
            multiply(pe, self.st, 0, h, ps[0:64, 4, :], hh, hl, 2, col0=MLA_NOPE, m=MLA_ROPE)
            multiply(pe, self.st, 1, h, ps[:, 6, :], hh, hl, 0)
            slot, k, width, _ = self.st.slabs[2]
            pe.wait_ge(s.lo_done[slot], self.st.use(2, h) + 1)
            for b in range(TB):
                tok = slice(b * P, (b + 1) * P)
                for j in range(k):
                    w = slice(j * width, (j + 1) * width)
                    end = product(pe, ps[:, 7, tok], hh[:, j, tok], hl[:, j, tok], wh[:, slot, w], wl[:, slot, w],
                                  j == 0, j == k - 1)
            end.then_inc(s.multiplied[slot], 1)

        def scores(self, pe, h):
            pe.wait_ge(s.m_lo, 4 * h + 4)
            pe.wait_ge(s.m_out_lo, h + SEED)
            for b in (3, 2, 0, 1):
                bank, off = self.WHERE[b]
                n = (b + 1) * P
                q, po = slice(b * P, n), ps[:, bank, off:off + n]
                product(pe, po, bh[:, self.QN, q], bl[:, self.QN, q], bh[:, self.KN, 0:n], bl[:, self.KN, 0:n],
                        True, False)
                pe.matmul(ps[:, bank, off + n - P:off + n], ident_r, mask_r, start=False, stop=False)
                product(pe, po, bh[0:64, self.QR, q], bl[0:64, self.QR, q], hh[0:64, 5, 0:n], hl[0:64, 5, 0:n],
                        False, True).then_inc(s.m_scores, 1)

        def values(self, pe, h):
            pe.wait_ge(s.m_combined, 4 * h + 4)
            attended(pe.transpose, self.prob, s.m_at)
            pe.wait_ge(s.m_at_lo, 3 * h + 3)
            for kt in range(TB):
                t, off = TRI[kt]
                w, k = slice(off, off + (TB - kt) * P), slice(kt * P, (kt + 1) * P)
                end = product(pe, ps[:, 3, kt * P:T], bh[:, self.V_, k], bl[:, self.V_, k],
                              bh[:, self.A_ + t, w], bl[:, self.A_ + t, w], kt == 0, kt == TB - 1)
            end.then_inc(s.m_pv, 1)

        def turn(self, pe, h):
            pe.wait_ge(s.m_raw, h + 1)
            pe.matmul(ps[:, 4, :], rot2[0:64, :], tmp[0:64, 0, :], start=True, stop=True).then_inc(s.m_rot, 1)

        def tensor(self, pe):
            pe.wait_ge(s.kvq_lo, 6)
            self.project(pe, 0)
            self.turn(pe, 0)
            with loop(pe, HEADS - 1) as h:
                self.scores(pe, h)
                self.project(pe, h + 1)
                self.values(pe, h)
                self.turn(pe, h + 1)
            self.scores(pe, HEADS - 1)
            self.values(pe, HEADS - 1)

        def exps(self, act, h):
            for n, b in enumerate((3, 2, 0, 1)):
                act.wait_ge(s.m_negmax, 4 * h + MAXED[b])
                bank, off = self.WHERE[b]
                w = (b + 1) * P
                act.activation(self.prob[:, POFF[b]:POFF[b] + w], ps[:, bank, off:off + w], ACT.Exp,
                               bias=nm[:, n:n + 1], scale=self.scale,
                               accum_out=den[:, n:n + 1]).then_inc(s.m_exp, 1)

        def raw(self, act, h):
            wait_product(act, self.st, 0, h)
            act.activation(tmp[0:64, 0, :], ps[0:64, 4, :], ACT.Copy).then_inc(s.m_raw, 1)

        def probs_hi(self, act, h):
            for b in range(3):
                act.wait_ge(s.m_at, 3 * h + b + 1)
                act.activation(bh[:, self.A_ + b, 0:TRI_W[b]], ps[:, b, 0:TRI_W[b]], ACT.Copy).then_inc(s.m_at_hi, 1)

        def nope_hi(self, act, h):
            act.activation(bh[:, self.QN, :], ps[:, 5, :], ACT.Copy).then_inc(s.m_hi, 1)
            wait_product(act, self.st, 1, h)
            act.activation(bh[:, self.KN, :], ps[:, 6, :], ACT.Copy).then_inc(s.m_hi, 1)

        def rest_hi(self, act, h):
            wait_product(act, self.st, 2, h)
            act.activation(bh[:, self.V_, :], ps[:, 7, :], ACT.Copy).then_inc(s.m_hi, 1)
            act.wait_ge(s.m_rope, 3 * h + 3)
            act.activation(bh[0:64, self.QR, :], tmp[0:64, 0, :], ACT.Copy).then_inc(s.m_hi, 1)

        def out_hi(self, act, h):
            act.wait_ge(s.m_pv, h + 1)
            act.activation(tile(bh, h), ps[:, 3, :], ACT.Copy).then_inc(s.m_out_hi, 1)

        def scalar(self, act):
            self.raw(act, 0)
            self.nope_hi(act, 0)
            self.rest_hi(act, 0)
            for slab in next_slabs(self.st, 0):
                split_hi(act, slab)

            def body(h, slabs):
                self.exps(act, h)
                self.raw(act, h + 1)
                for slab in slabs:
                    split_hi(act, slab)
                self.probs_hi(act, h)
                self.nope_hi(act, h + 1)
                self.out_hi(act, h)
                self.rest_hi(act, h + 1)
            with loop(act, HEADS - 2) as h:
                body(h, next_slabs(self.st, h + 1))
            body(HEADS - 2, last_slabs(self.st))
            self.exps(act, HEADS - 1)
            self.probs_hi(act, HEADS - 1)
            self.out_hi(act, HEADS - 1)

        def softmax(self, dve, h):
            for n, b in enumerate((3, 2, 0, 1)):
                bank, off = self.WHERE[b]
                dve.wait_ge(s.m_scores, 4 * h + self.SCORED[b])
                dve.reduce_max(mx[:, n:n + 1], ps[:, bank, off:off + (b + 1) * P], axis=AX_X).then_inc(s.m_max, 1)
                dve.wait_ge(s.m_max, 4 * h + n + 1)
                dve.tensor_scalar(nm[:, n:n + 1], mx[:, n:n + 1], -self.scale, None, ALU.mult).then_inc(s.m_negmax, 1)
            for n, b in enumerate((3, 2, 0, 1)):
                r = slice(POFF[b], POFF[b] + (b + 1) * P)
                dve.wait_ge(s.m_exp, 4 * h + n + 1)
                dve.reciprocal(inv[:, n:n + 1], den[:, n:n + 1]).then_inc(s.m_inv, 1)
                dve.wait_ge(s.m_inv, 4 * h + n + 1)
                dve.tensor_scalar(self.prob[:, r], self.prob[:, r], inv[:, n:n + 1], None,
                                  ALU.mult).then_inc(s.m_combined, 1)

        def low(self, dve, h, n, t, src, rows=P):
            dve.wait_ge(s.m_hi, 4 * h + n + 1)
            dve.tensor_tensor(bl[0:rows, t, :], src, bh[0:rows, t, :].bitcast(F32), ALU.subtract).then_inc(s.m_lo, 1)

        def before_out(self, dve, h):
            self.low(dve, h, 0, self.QN, ps[:, 5, :])
            self.low(dve, h, 1, self.KN, ps[:, 6, :])

        def behind_out(self, dve, h):
            dve.wait_ge(s.m_rot, h + 1)
            dve.tensor_tensor(tmp[0:64, 1, :], ps[0:64, 4, :], Latents.sin, ALU.mult).then_inc(s.m_rope, 1)
            dve.tensor_tensor(tmp[0:64, 0, :], tmp[0:64, 0, :], Latents.cos, ALU.mult).then_inc(s.m_rope, 1)
            dve.wait_ge(s.m_rope, 3 * h + 2)
            dve.tensor_tensor(tmp[0:64, 0, :], tmp[0:64, 0, :], tmp[0:64, 1, :], ALU.add).then_inc(s.m_rope, 1)
            self.low(dve, h, 2, self.V_, ps[:, 7, :])
            self.low(dve, h, 3, self.QR, tmp[0:64, 0, :], rows=64)

        def probs_lo(self, dve, h):
            for b in range(3):
                dve.wait_ge(s.m_at_hi, 3 * h + b + 1)
                w = slice(0, TRI_W[b])
                dve.tensor_tensor(bl[:, self.A_ + b, w], ps[:, b, w], bh[:, self.A_ + b, w].bitcast(F32),
                                  ALU.subtract).then_inc(s.m_at_lo, 1)

        def out_lo(self, dve, h):
            dve.wait_ge(s.m_out_hi, h + 1)
            dve.tensor_tensor(tile(bl, h), ps[:, 3, :], tile(bh, h).bitcast(F32), ALU.subtract).then_inc(s.m_out_lo, 1)

        def vector(self, dve):
            self.before_out(dve, 0)
            self.behind_out(dve, 0)
            with loop(dve, HEADS - 1) as h:
                self.softmax(dve, h)
                self.probs_lo(dve, h)
                self.before_out(dve, h + 1)
                self.out_lo(dve, h)
                self.behind_out(dve, h + 1)
            self.softmax(dve, HEADS - 1)
            self.probs_lo(dve, HEADS - 1)
            self.out_lo(dve, HEADS - 1)

        def gpsimd(self, pool):
            split_lo_stage(pool, self.st)

        def ready(self, pe, k):
            pe.wait_ge(s.m_out_lo, SEED + k + 1)

    CUM = [wh[0:64, 3, 0:T], wh[0:64, 3, T:2 * T], wl[0:64, 3, T:T + 256]]
    CUM_G = [bh[0:64, 15, :], bl[0:64, 15, :], wl[0:64, 3, 0:256]]
    neg_cum, dt_nat = stg[:, 3, 0:P], stg[:, 3, P:2 * P]
    exp_a = sm[0:SSD_H, 63:64]

    class StepSizes:

        def __init__(self, st, h):
            self.st, self.h = st, h

        def tensor(self, pe):
            multiply(pe, self.st, 0, 0, ps[0:SSD_H, 0, :], hh, hl, 0, m=SSD_H, ready=lambda j: self.h.ready(pe, j))
            pe.wait_ge(s.cum_done, 4)
            for r in range(TB):
                row, off = TRI[r]
                pe.transpose(ps[:, 1, r * SSD_H:(r + 1) * SSD_H], xT[0:SSD_H, row, off:off + P],
                             ident[0:SSD_H, 0:SSD_H])
                end = pe.transpose(ps[:, 1, P + r * SSD_H:P + (r + 1) * SSD_H], tmp[0:SSD_H, 0, r * P:(r + 1) * P],
                                   ident[0:SSD_H, 0:SSD_H])
            end.then_inc(s.cum_t, 1)

        def scalar(self, act):
            for slab in last_slabs(self.st):
                split_hi(act, slab)
            act.activation(exp_a, v("A_log")[0:SSD_H], ACT.Exp).then_inc(s.dt_exp, 1)
            act.wait_ge(s.dt_done, 2)
            act.activation(tmp[0:SSD_H, 1, :], tmp[0:SSD_H, 1, :], ACT.Exp, scale=-1.0).then_inc(s.dt_exp, 1)

        def vector(self, dve):
            n = [0]

            def link(instruction):
                n[0] += 1
                instruction.then_inc(s.dt_done, 1)
                dve.wait_ge(s.dt_done, n[0])
            x, e, w, w2, q, one = (tmp[0:SSD_H, t, :] for t in range(6))
            wait_product(dve, self.st, 0, 0)
            link(dve.tensor_scalar(x, ps[0:SSD_H, 0, :], v("dt_bias")[0:SSD_H], None, ALU.add))
            link(dve.scalar_tensor_tensor(e, x, -1.0, x, ALU.mult, ALU.max))
            dve.wait_ge(s.dt_exp, 2)
            link(dve.tensor_scalar(w2, e, 2.0, None, ALU.add))
            link(dve.reciprocal(w, w2))
            link(dve.tensor_tensor(w, w, e, ALU.mult))
            link(dve.tensor_tensor(w2, w, w, ALU.mult))
            link(dve.tensor_scalar(q, w2, 1.0 / 17, None, ALU.mult))
            for k in (15, 13, 11, 9, 7, 5, 3):
                link(dve.scalar_tensor_tensor(q, q, 1.0 / k, w2, ALU.add, ALU.mult))
            link(dve.scalar_tensor_tensor(q, q, 1.0, w, ALU.add, ALU.mult))
            link(dve.tensor_scalar(x, x, 0.0, None, ALU.max))
            link(dve.scalar_tensor_tensor(x, q, 2.0, x, ALU.mult, ALU.add))
            link(dve.tensor_scalar(e, x, exp_a, -1.0, ALU.mult, ALU.mult))
            link(dve.memset(one, 1.0))
            for r in range(TB):
                row, off = TRI[r]
                dve.tensor_tensor_scan(xT[0:SSD_H, row, off:off + T - r * P], one[:, r * P:T], e[:, r * P:T],
                                       0.0, ALU.mult, ALU.add).then_inc(s.cum_done, 1)
            dve.wait_ge(s.cum_done, 4)
            for p in range(3):
                src = xT[0:SSD_H, p, 0:TRI_W[p]]
                link(dve.tensor_copy(CUM[p][0:SSD_H], src))
                link(dve.tensor_tensor(CUM[p][SSD_H:2 * SSD_H], src, CUM[p][0:SSD_H].bitcast(F32), ALU.subtract))
            dve.wait_ge(s.cum_t, 1)
            dve.tensor_scalar(neg_cum, ps[:, 1, 0:P], -1.0, None, ALU.mult).then_inc(s.cum_n, 1)
            dve.tensor_copy(dt_nat, ps[:, 1, P:2 * P]).then_inc(s.cum_n, 1)
            dve.wait_ge(s.cum_n, 2)

        def gpsimd(self, pool):
            for slab in last_slabs(self.st):
                split_lo(pool, slab)

    class Ssd:
        B_, C_, X_, W_ = 8, 9, 10, 12
        decay = xT[:, 0:3, :]
        xs = [xT[:, 3, :], xT[:, 4, :]]
        zs = [xT[:, 5, :], xT[:, 6, :]]
        y = [xT[:, 7, :], tmp[:, 0, :]]

        def __init__(self, st, half):
            self.st, self.g0 = st, GROUPS // 2 * half

        def project(self, pe, i, pos):
            j = i + self.g0
            if pos in (1, 2):
                pe.wait_ge(s.z_silu, 2 * j + (SEED + pos - 2))
            else:
                pe.wait_ge(s.sc_conv, 4 * j + (SEED + max(0, pos - 2)))
            multiply(pe, self.st, pos, i, ps[:, pos % 3, :], hh, hl, 0)

        def cb_products(self, pe, i):
            j = i + self.g0
            pe.wait_ge(s.bc_lo, 2 * j + 2)
            pe.wait_ge(s.x_lo, 2 * j + 2)
            for r in (0, 1, 3, 2):
                row, off = TRI[r]
                k = slice(r * P, (r + 1) * P)
                end = product(pe, ps[:, 3 + row, off:off + T - r * P], bh[:, self.B_, k], bl[:, self.B_, k],
                              bh[:, self.C_, r * P:T], bl[:, self.C_, r * P:T], True, True)
                if r != 1:
                    end.then_inc(s.cb_done, 1)

        def decays(self, pe, i, k):
            j = i + self.g0
            if k == 0:
                pe.wait_ge(s.cb_copied, 3 * j + 3)
                pe.wait_ge(s.g_sel, 3 * j + 3)
            else:
                pe.wait_ge(s.e_done, 16 * j + 4 * k)
            for r in (0, 1, 3, 2):
                row, off = TRI[r]
                pe.matmul(ps[:, 3 + row, off:off + T - r * P], sel[0:64, k, :], CUM_G[row][:, off:off + T - r * P],
                          start=True, stop=False)
                end = pe.matmul(ps[:, 3 + row, off:off + P], mask_r, ident_r, start=False, stop=True)
                if r != 1:
                    end.then_inc(s.decay_done, 1)

        def outputs(self, pe, i, k):
            j = i + self.g0
            pe.wait_ge(s.w_lo, 12 * j + (3 * k + 3 + SEED))
            pe.wait_ge(s.y_copied, 4 * j + (k + SEED))
            for r in range(TB):
                row, off = TRI[r]
                c = (r % 2) * 256 + k * PD
                x = slice(c, c + PD)
                w = slice(off, off + T - r * P)
                end = product(pe, ps[0:PD, 6, r * P:T], bh[:, self.X_ + r // 2, x], bl[:, self.X_ + r // 2, x],
                              bh[:, self.W_ + row, w], bl[:, self.W_ + row, w], r == 0, r == TB - 1)
            end.then_inc(s.y_done, 1)

        def group_sums(self, pe, i):
            j = i + self.g0
            for p in range(2):
                pe.wait_ge(s.y_sq, 2 * j + p + 1)
                for b in range(TB):
                    end = pe.matmul(ps[:, 7, b:b + 1], tmp[:, 5, b * P:(b + 1) * P], ones[:, 0:1],
                                    start=p == 0 and b == 0, stop=p == 1, skip_group_check=True)
                end.then_inc(s.y_stat, 1)

        def group_spread(self, pe, i):
            pe.wait_ge(s.y_diag, i + self.g0 + 1)
            pe.matmul(ps[:, 7, :], ones, diag[:], start=True, stop=True).then_inc(s.y_bc, 1)

        def turn_x(self, pe, i):
            j = i + self.g0
            for c in range(TB):
                for p in range(2):
                    pe.wait_ge(s.sc_silu, 4 * j + 3 + p)
                    o = (c % 2) * 256 + p * P
                    end = pe.transpose(ps[:, 3 + c // 2, o:o + P], self.xs[p][:, c * P:(c + 1) * P], ident)
                if c % 2:
                    end.then_inc(s.x_nat, 1)

        def tensor(self, pe):
            def body(i, group, ahead):
                if group:
                    self.cb_products(pe, i)
                    self.decays(pe, i, 0)
                for k in range(HPG):
                    if ahead:
                        self.project(pe, i + 1, k)
                    if group:
                        self.outputs(pe, i, k)
                        if k + 1 < HPG:
                            self.decays(pe, i, k + 1)
                if ahead:
                    self.project(pe, i + 1, 4)
                if group:
                    self.group_sums(pe, i)
                if ahead:
                    self.project(pe, i + 1, 5)
                    self.turn_x(pe, i + 1)
                if group:
                    self.group_spread(pe, i)
            pe.wait_ge(s.cum_n, 2)
            body(-1, False, True)
            with loop(pe, 3) as i:
                body(i, True, True)
            body(3, True, False)

        def scaled(self, act, i, n):
            j = i + self.g0
            wait_product(act, self.st, n, i)
            if n >= 2:
                act.wait_ge(s.bc_lo, 2 * j + n - 1)
            elif not (isinstance(j, int) and j == 0):
                act.wait_ge(s.sc_silu, 4 * j)
            act.activation(tmp[:, 1 + 2 * (n % 2), :], ps[:, n % 3, :], ACT.Identity, bias=self.conv_col(i, n, 4),
                           scale=self.conv_col(i, n, 3)).then_inc(s.sc_scaled, 1)

        def conv_col(self, i, n, tap):
            j = i + self.g0
            at, step = ((16, 1), (24, 1), (0, 2), (1, 2))[n]
            return v("ssd_b", step * j + at) if tap == 4 else v("ssd_w", step * j + (tap * 32 + at))

        def gate(self, act, i, n):
            j = i + self.g0
            act.wait_ge(s.sc_conv, 4 * j + (SEED + n + 1))
            t = 1 + 2 * (n % 2)
            act.activation(tmp[:, t + 1, :], tmp[:, t, :], ACT.Tanh).then_inc(s.sc_gate, 1)

        def bc_high(self, act, i, n):
            act.wait_ge(s.sc_silu, 4 * (i + self.g0) + n + 1)
            act.activation(bh[:, self.B_ + n, :], tmp[:, 1 + 2 * n, :], ACT.Copy).then_inc(s.bc_hi, 1)

        def z_gates(self, act, i, n):
            wait_product(act, self.st, 4 + n, i)
            act.wait_ge(s.sc_silu, 4 * (i + self.g0) + 3 + n)
            act.activation(tmp[:, 2 + 2 * n, :], ps[:, 1 + n, :], ACT.Tanh, scale=0.5).then_inc(s.z_gate, 1)

        def x_high(self, act, i):
            for c in range(2):
                act.wait_ge(s.x_nat, 2 * (i + self.g0) + c + 1)
                act.activation(bh[:, self.X_ + c, :], ps[:, 3 + c, :], ACT.Copy).then_inc(s.x_hi, 1)

        def cb_copy(self, act, i):
            for p in range(3):
                act.wait_ge(s.cb_done, 3 * (i + self.g0) + p + 1)
                act.activation(cb[:, p, 0:TRI_W[p]], ps[:, 3 + p, 0:TRI_W[p]], ACT.Copy).then_inc(s.cb_copied, 1)

        def head_exps(self, act, i, k):
            j = i + self.g0
            act.wait_ge(s.w_lo, 12 * j + (3 * k + SEED))
            for n, r in enumerate((0, 1, 3, 2)):
                row, off = TRI[r]
                act.wait_ge(s.decay_done, 12 * j + (SEED + 3 * k + (1, 2, 2, 3)[n]))
                w = slice(off, off + T - r * P)
                c = 4 * j + (r * SSD_H + k)
                bias = neg_cum[:, c:c + 1] if isinstance(c, int) else stg[:, 3, bass.ds(c, 1)]
                act.activation(self.decay[:, row, w], ps[:, 3 + row, w], ACT.Exp, bias=bias).then_inc(s.e_done, 1)

        def w_high(self, act, i, k):
            j = i + self.g0
            for p in range(3):
                act.wait_ge(s.w_done, 16 * j + (4 * k + (1, 3, 4)[p]))
                act.activation(bh[:, self.W_ + p, 0:TRI_W[p]], self.decay[:, p, 0:TRI_W[p]],
                               ACT.Copy).then_inc(s.w_hi, 1)

        def y_copy(self, act, i, k):
            j = i + self.g0
            act.wait_ge(s.y_done, 4 * j + k + 1)
            act.wait_ge(s.y_lo, 2 * j + SEED)
            r = (k % 2) * PD
            act.activation(self.y[k // 2][r:r + PD, :], ps[0:PD, 6, :], ACT.Copy).then_inc(s.y_copied, 1)

        def y_square(self, act, i, p):
            j = i + self.g0
            act.wait_ge(s.y_gate, 2 * j + p + 1)
            act.wait_ge(s.y_stat, 2 * j + (SEED + p))
            act.activation(tmp[:, 5, :], self.y[p], ACT.Square).then_inc(s.y_sq, 1)

        def y_high(self, act, i):
            for p in range(2):
                act.wait_ge(s.y_norm, 2 * (i + self.g0) + p + 1)
                act.activation(tile(bh, 2 * i + p), self.y[p], ACT.Copy).then_inc(s.y_hi, 1)

        def scalar(self, act):
            def body(i, group, ahead, slabs=()):
                slabs = list(slabs)

                def split(n=1):
                    for _ in range(n):
                        if slabs:
                            split_hi(act, slabs.pop(0))
                if group:
                    self.cb_copy(act, i)
                for k in range(HPG):
                    if group:
                        self.head_exps(act, i, k)
                        self.w_high(act, i, k)
                    if ahead:
                        if k > 0:
                            self.gate(act, i + 1, k - 1)
                        if k > 1:
                            self.bc_high(act, i + 1, k - 2)
                        self.scaled(act, i + 1, k)
                        split()
                    if group:
                        self.y_copy(act, i, k)
                if ahead:
                    self.gate(act, i + 1, 3)
                    self.z_gates(act, i + 1, 0)
                    split()
                if group:
                    self.y_square(act, i, 0)
                    self.y_square(act, i, 1)
                if ahead:
                    self.z_gates(act, i + 1, 1)
                    split(len(slabs))
                    self.x_high(act, i + 1)
                if group:
                    self.y_high(act, i)
            body(-1, False, True, next_slabs(self.st, 0))
            with loop(act, 2) as i:
                body(i, True, True, next_slabs(self.st, i + 1))
            body(2, True, True, last_slabs(self.st))
            body(3, True, False)

        def select(self, dve, i):
            j = i + self.g0
            dve.wait_ge(s.decay_done, 12 * j + SEED)
            m = gmask[:, j:j + 1] if isinstance(j, int) else gmask[:, bass.ds(j, 1)]
            for p in range(3):
                dve.tensor_scalar(CUM_G[p], CUM[p].bitcast(F32), m, None, ALU.mult).then_inc(s.g_sel, 1)

        def weights(self, dve, i, k):
            j = i + self.g0
            if k == 0:
                dve.wait_ge(s.cb_copied, 3 * j + 3)
            for n, r in enumerate((0, 1, 3, 2)):
                row, off = TRI[r]
                w = slice(off, off + T - r * P)
                c = 4 * j + (r * SSD_H + k)
                dt = dt_nat[:, c:c + 1] if isinstance(c, int) else stg[:, 3, bass.ds(c + P, 1)]
                dve.wait_ge(s.e_done, 16 * j + 4 * k + n + 1)
                dve.scalar_tensor_tensor(self.decay[:, row, w], self.decay[:, row, w], dt, cb[:, row, w],
                                         ALU.mult, ALU.mult).then_inc(s.w_done, 1)
            for p in range(3):
                dve.wait_ge(s.w_hi, 12 * j + 3 * k + p + 1)
                w = slice(0, TRI_W[p])
                dve.tensor_tensor(bl[:, self.W_ + p, w], self.decay[:, p, w], bh[:, self.W_ + p, w].bitcast(F32),
                                  ALU.subtract).then_inc(s.w_lo, 1)

        def taps(self, dve, i, n):
            j = i + self.g0
            x, y = ps[:, n % 3, :], tmp[:, 1 + 2 * (n % 2), :]
            dve.wait_ge(s.sc_scaled, 4 * j + n + 1)
            for d in (1, 2, 3):
                op = dve.scalar_tensor_tensor(y[:, d:T], x[:, 0:T - d], self.conv_col(i, n, 3 - d), y[:, d:T],
                                              ALU.mult, ALU.add)
                op.then_inc(s.sc_conv if d == 3 else s.sc_tap, 1)
                if d < 3:
                    dve.wait_ge(s.sc_tap, 8 * j + 2 * n + d)

        def silu(self, dve, i, n):
            t = 1 + 2 * (n % 2)
            dve.wait_ge(s.sc_gate, 4 * (i + self.g0) + n + 1)
            dve.scalar_tensor_tensor(tmp[:, t, :] if n < 2 else self.xs[n - 2], tmp[:, t + 1, :], 1.0, tmp[:, t, :],
                                     ALU.add, ALU.mult).then_inc(s.sc_silu, 1)

        def bc_low(self, dve, i, n):
            dve.wait_ge(s.bc_hi, 2 * (i + self.g0) + n + 1)
            dve.tensor_tensor(bl[:, self.B_ + n, :], tmp[:, 1 + 2 * n, :], bh[:, self.B_ + n, :].bitcast(F32),
                              ALU.subtract).then_inc(s.bc_lo, 1)

        def z_silus(self, dve, i, n):
            dve.wait_ge(s.z_gate, 2 * (i + self.g0) + n + 1)
            dve.scalar_tensor_tensor(self.zs[n], tmp[:, 2 + 2 * n, :], 1.0, ps[:, 1 + n, :],
                                     ALU.add, ALU.mult).then_inc(s.z_silu, 1)

        def x_low(self, dve, i):
            for c in range(2):
                dve.wait_ge(s.x_hi, 2 * (i + self.g0) + c + 1)
                dve.tensor_tensor(bl[:, self.X_ + c, :], ps[:, 3 + c, :], bh[:, self.X_ + c, :].bitcast(F32),
                                  ALU.subtract).then_inc(s.x_lo, 1)

        def skip_and_gate(self, dve, i, p):
            j = i + self.g0
            y = self.y[p]
            dve.wait_ge(s.y_copied, 4 * j + (SEED + 2 * p + 2))
            dve.scalar_tensor_tensor(y, self.xs[p], v("ssd_D", 2 * j + p), y, ALU.mult, ALU.add).then_inc(s.y_skip, 1)
            dve.wait_ge(s.y_skip, 2 * j + p + 1)
            dve.scalar_tensor_tensor(y, y, 0.5, self.zs[p], ALU.mult, ALU.mult).then_inc(s.y_gate, 1)

        def group_var(self, dve, i):
            j = i + self.g0
            dve.wait_ge(s.y_stat, 2 * j + (SEED + 2))
            dve.tensor_scalar(ovar, ps[:, 7, 0:4], 1.0 / (2 * P), LN_EPS, ALU.mult, ALU.add).then_inc(s.y_var, 1)

        def group_diag(self, dve, i):
            dve.wait_ge(s.y_rstd, i + self.g0 + 1)
            dve.tensor_tensor(diag[:].rearrange("p (b t) -> p b t", b=TB),
                              ident.rearrange("p (a t) -> p a t", a=1).to_broadcast([P, TB, P]),
                              orstd.rearrange("p (b a) -> p b a", a=1).to_broadcast([P, TB, P]),
                              ALU.mult).then_inc(s.y_diag, 1)

        def group_norm(self, dve, i):
            j = i + self.g0
            dve.wait_ge(s.y_bc, j + 1)
            for p in range(2):
                dve.scalar_tensor_tensor(self.y[p], self.y[p], v("ssd_norm", 2 * j + p), ps[:, 7, :],
                                         ALU.mult, ALU.mult).then_inc(s.y_norm, 1)
            for p in range(2):
                dve.wait_ge(s.y_hi, 2 * j + p + 1)
                dve.tensor_tensor(tile(bl, 2 * i + p), self.y[p], tile(bh, 2 * i + p).bitcast(F32),
                                  ALU.subtract).then_inc(s.y_lo, 1)

        def vector(self, dve):
            def body(i, group, ahead):
                if group:
                    self.select(dve, i)
                for k in range(HPG):
                    if group:
                        self.weights(dve, i, k)
                        if k == 2:
                            self.skip_and_gate(dve, i, 0)
                    if ahead:
                        if k > 0:
                            self.silu(dve, i + 1, k - 1)
                        if k > 1:
                            self.bc_low(dve, i + 1, k - 2)
                        self.taps(dve, i + 1, k)
                if group:
                    self.skip_and_gate(dve, i, 1)
                if ahead:
                    self.silu(dve, i + 1, 3)
                    self.z_silus(dve, i + 1, 0)
                if group:
                    self.group_var(dve, i)
                if ahead:
                    self.z_silus(dve, i + 1, 1)
                if group:
                    self.group_diag(dve, i)
                if ahead:
                    self.x_low(dve, i + 1)
                if group:
                    self.group_norm(dve, i)
            body(-1, False, True)
            with loop(dve, 3) as i:
                body(i, True, True)
            body(3, True, False)

        def gpsimd(self, pool):
            for slab in next_slabs(self.st, 0):
                split_lo(pool, slab)

            def body(i, slabs):
                for slab in slabs[:5]:
                    split_lo(pool, slab)
                pool.wait_ge(s.y_var, i + self.g0 + 1)
                pool.tensor_tensor(orstd, ovar, half4, ALU.pow).then_inc(s.y_rstd, 1)
                for slab in slabs[5:]:
                    split_lo(pool, slab)
            with loop(pool, 2) as i:
                body(i, next_slabs(self.st, i + 1))
            body(2, last_slabs(self.st))
            body(3, [])

        def ready(self, pe, k):
            pe.wait_ge(s.y_lo, SEED + 2 * self.g0 + k + 1)

    class Start:

        def sync(self, sp):
            for j in range(0, DT_, 4):
                sp.dma_start(xT[:, j:j + 4, :], a["xT"][j * P:(j + 4) * P, :].rearrange("(k p) t -> p k t", p=P))\
                    .then_inc(s.x_in, 16)
            sp.dma_start(con[:], a["consts"][:, 0:C["mask"]]).then_inc(s.const_in, 16)
            sp.dma_start(vec[:], a["vecs"]).then_inc(s.const_in, 16)
            sp.dma_start(acc[:, 0:2, :].rearrange("p a t -> p (a t)")[:, 0:P + HPG * P],
                         a["consts"][:, C["mask"]:C["cos"]]).then_inc(s.const_in, 16)
            sp.dma_start(cb[:, 0:2, :].rearrange("p a t -> p (a t)"),
                         a["consts"][:, C["cos"]:C["cos"] + 2 * T]).then_inc(s.const_in, 16)
            sp.dma_start(gmask[:], a["consts"][0:64, C["gmask"]:C["gmask"] + GROUPS]).then_inc(s.const_in, 16)
            sp.dma_start(positions[:], a["positions_2"].to_broadcast([64, T])).then_inc(s.const_in, 16)
            for n, x in enumerate(("attn_lambda_q1", "attn_lambda_k1", "attn_lambda_q2", "attn_lambda_k2")):
                sp.dma_start(tmp[:, n, 0:64], a[x].to_broadcast([P, 64])).then_inc(s.const_in, 16)

        def vector(self, dve):
            dve.memset(half4, -0.5).then_inc(s.lam_in, 1)
            dve.wait_ge(s.const_in, 10 * 16)
            dve.tensor_copy(ident_r, ident).then_inc(s.const_r, 1)
            dve.tensor_copy(cr[:, P:], acc[:, 0:2, :].rearrange("p a t -> p (a t)")[:, 0:P + HPG * P])\
                .then_inc(s.const_r, 1)
            for n in range(2):
                dve.tensor_tensor(tmp[:, 2 * n, 0:64], tmp[:, 2 * n, 0:64], tmp[:, 2 * n + 1, 0:64],
                                  ALU.mult).then_inc(s.lam_sum, 1)
                dve.wait_ge(s.lam_sum, 2 * n + 1)
                dve.reduce_sum(lam2[:, n:n + 1], tmp[:, 2 * n, 0:64], axis=AX_X).then_inc(s.lam_sum, 1)
            dve.tensor_scalar(vec[:, V["ssd_w"]:V["ssd_b"] + 32], vec[:, V["ssd_w"]:V["ssd_b"] + 32], 0.5, None,
                              ALU.mult).then_inc(s.lam_done, 1)
            dve.tensor_scalar(subg, v("subln"), 1.0 - LAMBDA_INIT, None, ALU.mult).then_inc(s.lam_done, 1)
            dve.wait_ge(s.lam_exp, 1)
            dve.scalar_tensor_tensor(lam, lam2[:, 1:2], -LAMBDA_INIT, lam2[:, 0:1],
                                     ALU.add, ALU.subtract).then_inc(s.lam_done, 1)
            dve.wait_ge(s.lam_done, 3)

        def scalar(self, act):
            act.wait_ge(s.lam_sum, 4)
            act.activation(lam2, lam2, ACT.Exp).then_inc(s.lam_exp, 1)
            for slab in first_slabs(stream[0]):
                split_hi(act, slab)

        def tensor(self, pe):
            pe.wait_ge(s.const_r, 2)
            pe.wait_ge(s.lam_done, 3)

        def gpsimd(self, pool):
            pool.wait_ge(s.lam_in, 1)
            for slab in first_slabs(stream[0]):
                split_lo(pool, slab)

    def x_loaded(eng, j):
        eng.wait_ge(s.x_in, 32)

    class Finish:
        def __init__(self, waits):
            self.waits = waits

        def sync(self, sp):
            for j in range(DT_):
                self.waits(sp, j)
                sp.dma_start(out[j * P:(j + 1) * P, :], xT[:, j, :]).then_inc(s.out_done, 16)
            sp.wait_ge(s.out_done, 16 * DT_)

    steps = [Start()]

    def add(step):
        steps.append(step)
        return step

    x, h = x_loaded, None
    for section in sections:
        if section == "attention":
            h = add(PreNorm("mix_pre", 0, x))
            att = add(DiffAttention(st_att, h))
            d = add(Dense(st_o, bh, bl, 1, att.ready, "copy"))
            x = add(PostNorm("mix_post", 0, d)).done
        elif section == "conv":
            h = add(PreNorm("mix_pre", 1, x))
            hid = hidden_before[0]
            add(ShortConv(st_conv, h))
            d = add(Dense(st_cout, bh, bl, 1, hidden_ready(hid), "copy"))
            x = add(PostNorm("mix_post", 1, d)).done
        elif section.startswith("mlp"):
            layer = int(section[-1])
            h = add(PreNorm("mlp_pre", layer, x))
            for half in range(2):
                up, down = st_mlp[layer, half]
                hid = hidden_before[0]
                add(Up(up, h))
                d = add(Dense(down, bh, bl, 2, hidden_ready(hid), "copy" if half == 0 else "add"))
            x = add(PostNorm("mlp_post", layer, d)).done
        elif section == "split":
            h = add(SplitX(x))
        elif section.startswith("ffn"):
            layer = int(section[-1])
            for half in range(2):
                up, down = st_ffn[layer, half]
                hid = hidden_before[0]
                add(GatedUp(up, layer, half * FFN_HALVES[0], h))
                d = add(Dense(down, bh, bl, 2, hidden_ready(hid), "copy" if half == 0 else "add"))
            h = add(LayerNorm("ln_ffn_g", "ln_ffn_b", layer, d, last=section == sections[-1]))
            x = h.done
        elif section == "mla":
            add(Latents(st_lat, h))
            lat = add(LatentAttention(st_mla))
            d = add(Dense(st_mo, bh, bl, 1, lat.ready, "copy"))
            h = add(LayerNorm("ln_mix_g", "ln_mix_b", 1, d))
            x = h.done
        elif section == "ssd":
            add(StepSizes(st_dt, h))
            for half in range(2):
                ssd = add(Ssd(st_ssd[half][0], half))
                d = add(Dense(st_ssd[half][1], bh, bl, 1, ssd.ready, "copy" if half == 0 else "add"))
            h = add(LayerNorm("ln_mix_g", "ln_mix_b", 0, d, from_parts=True))
            x = h.done
    steps.append(Finish(x))


    with nc.Block() as block:

        @block.sync
        def _(sp):
            steps[0].sync(sp)
            load_slabs(sp)
            steps[-1].sync(sp)

        @block.gpsimd
        def _(pool):
            for sem in (s.bank_free, s.conv_read, s.acc_done, s.stat_used, s.squared, s.ot_lo, s.m_out_lo, s.sc_conv, s.z_silu, s.w_lo, s.decay_done,
                        s.y_copied, s.y_lo, s.y_stat, s.c_copied, s.conv_u, s.gated):
                pool.sem_inc(sem, SEED)
            for k in range(SLOTS):
                pool.sem_inc(s.lo_done[k], 1)
                pool.sem_inc(s.multiplied[k], 1)
            for step in steps[:-1]:
                step.gpsimd(pool)

        @block.scalar
        def _(act):
            for step in steps[:-1]:
                step.scalar(act)

        @block.vector
        def _(dve):
            for step in steps[:-1]:
                step.vector(dve)

        @block.tensor
        def _(pe):
            for step in steps[:-1]:
                step.tensor(pe)
    return ctx


NAMES = ["attn_w_qkv", "attn_w_o", "attn_lambda_q1", "attn_lambda_k1", "attn_lambda_q2", "attn_lambda_k2",
         "conv_w_in", "conv_w_out", "mlp_w_up", "mlp_w_down", "ssd_in_proj_2", "ssd_out_proj_2",
         "kv_down_proj_2", "kv_up_k_2", "kv_up_v_2", "q_down_proj_2", "q_up_proj_2", "attn_out_proj_2",
         "ffn_up_2", "ffn_down_2", "positions_2"]


def packed_vectors(x):
    at, n = vector_columns()
    rows = np.zeros((n, P), np.float32)

    def put(name, arr):
        arr = np.ascontiguousarray(arr).reshape(-1)
        k = -(-arr.size // P)
        rows[at[name]:at[name] + k].reshape(-1)[:arr.size] = arr
    put("mix_pre", x["norm_mixer_pre"])
    put("mix_post", x["norm_mixer_post"])
    put("mlp_pre", x["norm_mlp_pre"])
    put("mlp_post", x["norm_mlp_post"])
    put("conv_w", x["conv_w"])
    put("subln", x["attn_subln_g"])
    put("ssd_w", x["ssd_conv_w_2"])
    put("ssd_b", x["ssd_conv_b_2"])
    put("ssd_norm", x["ssd_norm_g_2"])
    put("ssd_D", np.repeat(x["ssd_D_2"], PD))
    put("A_log", np.tile(x["ssd_A_log_2"].reshape(-1), 2))
    put("dt_bias", np.tile(x["ssd_dt_bias_2"].reshape(-1), 2))
    put("kv_g", x["kv_norm_g_2"])
    put("q_g", x["q_norm_g_2"])
    put("ffn_w", x["ffn_conv_w_2"])
    put("ffn_b", x["ffn_conv_b_2"])
    put("ln_mix_g", x["ln_mix_g_2"])
    put("ln_mix_b", x["ln_mix_b_2"])
    put("ln_ffn_g", x["ln_ffn_g_2"])
    put("ln_ffn_b", x["ln_ffn_b_2"])
    inv = (1.0 / (np.float32(10000.0) ** (np.arange(0, MLA_ROPE, 2, dtype=np.float32) / MLA_ROPE))).astype(np.float32)
    put("inv_freq", np.concatenate([inv, inv]))
    return np.ascontiguousarray(rows.T)


def constants():
    at, n = constant_columns()
    c = np.zeros((P, n), np.float32)
    c[:, at["ident"]:at["ident"] + P] = np.eye(P)
    c[:, at["ones"]:at["ones"] + P] = 1.0
    r = np.zeros((P, P), np.float32)
    for base in (0, 64):
        for j in range(HALF_ROT):
            r[base + HALF_ROT + j, base + j] = -1.0
            r[base + j, base + HALF_ROT + j] = 1.0
    c[:, at["rot"]:at["rot"] + P] = r
    r = np.zeros((P, P), np.float32)
    for j in range(32):
        r[32 + j, j] = -1.0
        r[j, 32 + j] = 1.0
    c[:, at["rot2"]:at["rot2"] + P] = r
    q, k = np.meshgrid(np.arange(P), np.arange(P), indexing="ij")
    c[:, at["mask"]:at["mask"] + P] = np.where(k > q, NEG, 0.0)
    for h in range(HPG):
        for row in range(64):
            if row % HPG == h:
                c[row, at["sel"] + h * P:at["sel"] + (h + 1) * P] = 1.0
    pos = np.arange(T, dtype=np.float32)
    inv = (np.float32(500000.0) ** (-np.arange(0, 2 * HALF_ROT, 2, dtype=np.float32) / (2 * HALF_ROT))).astype(np.float32)
    ang = (pos[None, :] * inv[:, None]).astype(np.float32)
    cos, sin = np.ones((P, T), np.float32), np.zeros((P, T), np.float32)
    for base in (0, 64):
        for half in range(2):
            cos[base + half * HALF_ROT:base + (half + 1) * HALF_ROT] = np.cos(ang)
            sin[base + half * HALF_ROT:base + (half + 1) * HALF_ROT] = np.sin(ang)
    c[:, at["cos"]:at["cos"] + T] = cos
    c[:, at["sin"]:at["sin"] + T] = sin
    for g in range(GROUPS):
        for row in range(64):
            if (row % SSD_H) // HPG == g:
                c[row, at["gmask"] + g] = 1.0
    return c


def kernel(**inputs):
    from concourse import bacc
    from concourse.bass_utils import run_bass_kernel_spmd

    x = {k: np.asarray(w) for k, w in inputs.items()}
    arrays = {k: np.ascontiguousarray(x[k]) for k in NAMES}
    arrays["xT"] = np.ascontiguousarray(x["x"][0].T)
    arrays["vecs"] = packed_vectors(x)
    arrays["consts"] = constants()
    nc = bacc.Bacc("TRN2", target_bir_lowering=False, num_devices=1)
    aps = {k: nc.dram_tensor("in_" + k, w.shape, mybir.dt.from_np(w.dtype), kind="ExternalInput").ap()
           for k, w in arrays.items()}
    out = nc.dram_tensor("out", (D, T), F32, kind="ExternalOutput").ap()
    with program(nc, aps, out):
        pass
    r = run_bass_kernel_spmd(nc, [{"in_" + k: w for k, w in arrays.items()}], core_ids=[0])
    return np.ascontiguousarray(r.results[0]["out"].T)[None]
```
